# Optimizing a Trainium2 kernel written in Bass

```python
import math
import jax, jax.numpy as jnp
from jax import lax
import numpy as np

D_MODEL = 2048
BATCH = 1
SEQ = 512
DEPTH = 1
DEC_BATCH = 8
DEC_SEQ = 8
PAST_LEN = 2048
PAGE_SIZE = 128

ATT_HEADS = 16
ATT_HEAD_DIM = 64
D_ATT = ATT_HEADS * ATT_HEAD_DIM
Q_BLOCK = 128
D_SSM = D_MODEL
SSM_HEAD_DIM = 64
SSM_HEADS = D_SSM // SSM_HEAD_DIM
SSM_GROUPS = 8
SSM_STATE = 128
CONV_WIDTH = 4
CONV_DIM = D_SSM + 2 * SSM_GROUPS * SSM_STATE
SSD_CHUNK = 128
PEER_HEADS = 8
N_KEYS = 128
N_EXPERTS = N_KEYS * N_KEYS
PK_DIM = 256
PK_HALF = PK_DIM // 2
PK_TOPK = 16
PEER_BLOCK = 128
IN_SIZES = (D_ATT, D_ATT, D_ATT, ATT_HEADS, D_SSM, CONV_DIM, SSM_HEADS, D_MODEL, D_MODEL)
N_IN = 3 * D_ATT + ATT_HEADS + D_SSM + CONV_DIM + SSM_HEADS + 2 * D_MODEL
DEEPNORM_ALPHA = (2 * DEPTH) ** 0.25
DEEPNORM_BETA = (8 * DEPTH) ** -0.25
NORM_EPS = 1e-5
CACHE_FORGET_BIAS = 7.0

kernel_name = 'fox_mamba2_peer_hybrid_step'

def layer_norm(x, g, b):
    xf = x.astype(jnp.float32)
    mu = jnp.mean(xf, -1, keepdims=True)
    var = jnp.mean(jnp.square(xf - mu), -1, keepdims=True)
    return ((xf - mu) * lax.rsqrt(var + NORM_EPS)).astype(x.dtype) * g + b

def split_in(u):
    offs, acc = [], 0
    for s in IN_SIZES[:-1]:
        acc += s
        offs.append(acc)
    return jnp.split(u, offs, axis=-1)

def mixer_inputs(x, w_in, b_fgate):
    bsz, l = x.shape[:2]
    q, k, v, fg, z, xbc, dt_raw, ga, gs = split_in(x @ w_in)
    shp = (bsz, l, ATT_HEADS, ATT_HEAD_DIM)
    logf = jax.nn.log_sigmoid(fg.astype(jnp.float32) + b_fgate)
    return q.reshape(shp), k.reshape(shp), v.reshape(shp), logf, z, xbc, dt_raw, ga, gs

def fox_prompt(q, k, v, logf):
    b, s, h, dh = q.shape
    scale = dh ** -0.5
    cum_t = jnp.transpose(lax.cumsum(logf, axis=1), (0, 2, 1))
    kpos = jnp.arange(s)

    def block(i):
        start = i * Q_BLOCK
        qb = lax.dynamic_slice_in_dim(q, start, Q_BLOCK, axis=1)
        cq = lax.dynamic_slice_in_dim(cum_t, start, Q_BLOCK, axis=2)
        logits = jnp.einsum('bqhd,bkhd->bhqk', qb, k).astype(jnp.float32) * scale
        logits = logits + cq[..., :, None] - cum_t[..., None, :]
        qpos = start + jnp.arange(Q_BLOCK)
        logits = jnp.where(kpos[None, :] <= qpos[:, None], logits, -jnp.inf)
        p = jax.nn.softmax(logits, axis=-1).astype(v.dtype)
        return jnp.einsum('bhqk,bkhd->bqhd', p, v)

    out = lax.map(block, jnp.arange(s // Q_BLOCK))
    return jnp.moveaxis(out, 0, 1).reshape(b, s, h, dh)

def fox_sample(q, k, v, logf, k_past, v_past, logf_past):
    l = q.shape[1]
    past = k_past.shape[1]
    scale = q.shape[-1] ** -0.5
    lp32 = logf_past.astype(jnp.float32)
    rev = lax.cumsum(lp32, axis=1, reverse=True) - lp32
    rev_t = jnp.transpose(rev, (0, 2, 1))
    cn_t = jnp.transpose(lax.cumsum(logf, axis=1), (0, 2, 1))
    lg_past = jnp.einsum('bqhd,bkhd->bhqk', q, k_past).astype(jnp.float32) * scale
    lg_past = lg_past + cn_t[..., :, None] + rev_t[..., None, :]
    lg_new = jnp.einsum('bqhd,bkhd->bhqk', q, k).astype(jnp.float32) * scale
    lg_new = lg_new + cn_t[..., :, None] - cn_t[..., None, :]
    causal = jnp.tril(jnp.ones((l, l), dtype=bool))
    lg_new = jnp.where(causal, lg_new, -jnp.inf)
    p = jax.nn.softmax(jnp.concatenate([lg_past, lg_new], axis=-1), axis=-1).astype(v.dtype)
    return (jnp.einsum('bhqk,bkhd->bqhd', p[..., :past], v_past)
            + jnp.einsum('bhqk,bkhd->bqhd', p[..., past:], v))

def causal_conv(xbc, buf, w, b):
    l = xbc.shape[1]
    xp = jnp.concatenate([buf.astype(xbc.dtype), xbc], axis=1)
    y = b
    for j in range(CONV_WIDTH):
        y = y + w[j] * xp[:, j:j + l]
    return jax.nn.silu(y), xp[:, l:]

def ssd(x, dt, a, bm, cm, h0):
    bsz, l = x.shape[:2]
    t = math.gcd(SSD_CHUNK, l)
    nc = l // t
    r = SSM_HEADS // SSM_GROUPS
    xc = (x * dt[..., None]).reshape(bsz, nc, t, SSM_GROUPS, r, SSM_HEAD_DIM)
    cs = lax.cumsum((dt * a).reshape(bsz, nc, t, SSM_GROUPS, r), axis=2)
    bc = bm.reshape(bsz, nc, t, SSM_GROUPS, SSM_STATE)
    cc = cm.reshape(bsz, nc, t, SSM_GROUPS, SSM_STATE)
    seg = cs[:, :, :, None] - cs[:, :, None, :]
    causal = jnp.tril(jnp.ones((t, t), dtype=bool))[:, :, None, None]
    decay = jnp.where(causal, jnp.exp(jnp.where(causal, seg, 0.0)), 0.0)
    cb = jnp.einsum('bctgn,bcsgn->bctsg', cc, bc)
    y_diag = jnp.einsum('bctsg,bctsgr,bcsgrp->bctgrp', cb, decay, xc)
    decay_end = jnp.exp(cs[:, :, -1:] - cs)
    states = jnp.einsum('bcsgn,bcsgr,bcsgrp->bcgrpn', bc, decay_end, xc)
    chunk_decay = jnp.exp(cs[:, :, -1])

    def step(h, inp):
        st, dec = inp
        return h * dec[..., None, None] + st, h

    h0g = h0.reshape(bsz, SSM_GROUPS, r, SSM_HEAD_DIM, SSM_STATE)
    h_fin, h_prev = lax.scan(step, h0g, (jnp.moveaxis(states, 1, 0), jnp.moveaxis(chunk_decay, 1, 0)))
    h_prev = jnp.moveaxis(h_prev, 0, 1)
    y_off = jnp.einsum('bctgn,bcgrpn,bctgr->bctgrp', cc, h_prev, jnp.exp(cs))
    y = (y_diag + y_off).reshape(bsz, l, SSM_HEADS, SSM_HEAD_DIM)
    return y, h_fin.reshape(bsz, SSM_HEADS, SSM_HEAD_DIM, SSM_STATE)

def mamba_branch(z, xbc, dt_raw, conv_buf, h0, conv_w, conv_b, dt_bias, a_log, d_skip, norm_w):
    bsz, l = z.shape[:2]
    xbc, new_buf = causal_conv(xbc, conv_buf, conv_w, conv_b)
    xs, bm, cm = jnp.split(xbc, [D_SSM, D_SSM + SSM_GROUPS * SSM_STATE], axis=-1)
    xs = xs.reshape(bsz, l, SSM_HEADS, SSM_HEAD_DIM)
    dt = jax.nn.softplus(dt_raw.astype(jnp.float32) + dt_bias)
    a = -jnp.exp(a_log.astype(jnp.float32))
    y, h_new = ssd(xs, dt, a, bm.reshape(bsz, l, SSM_GROUPS, SSM_STATE),
                   cm.reshape(bsz, l, SSM_GROUPS, SSM_STATE), h0.astype(jnp.float32))
    y = (y + d_skip[:, None] * xs).reshape(bsz, l, D_SSM) * jax.nn.silu(z)
    yg = y.reshape(bsz, l, SSM_GROUPS, D_SSM // SSM_GROUPS).astype(jnp.float32)
    yg = yg * lax.rsqrt(jnp.mean(jnp.square(yg), -1, keepdims=True) + NORM_EPS)
    return yg.reshape(bsz, l, D_SSM).astype(z.dtype) * norm_w, new_buf, h_new

def merge_branches(x, att, ssm, ga, gs, w_br_att, w_br_ssm, w_out, g, b):
    bsz, l = x.shape[:2]
    mixed = (jax.nn.sigmoid(ga) * (att.reshape(bsz, l, D_ATT) @ w_br_att)
             + jax.nn.sigmoid(gs) * (ssm @ w_br_ssm))
    return layer_norm(DEEPNORM_ALPHA * x + mixed @ w_out, g, b)

def peer(x, w_query, sub_keys, expert_u, expert_v):
    shp = x.shape
    xt = x.reshape(-1, D_MODEL)
    n = xt.shape[0]
    n_pad = -(-n // PEER_BLOCK) * PEER_BLOCK
    xt = jnp.pad(xt, ((0, n_pad - n), (0, 0)))

    def block(xb):
        tn = xb.shape[0]
        q = (xb @ w_query).reshape(tn, PEER_HEADS, 2, PK_HALF)
        s = jnp.einsum('thkd,hknd->thkn', q, sub_keys).astype(jnp.float32)
        top_s, top_i = lax.top_k(s, PK_TOPK)
        cand_s = (top_s[:, :, 0, :, None] + top_s[:, :, 1, None, :]).reshape(tn, PEER_HEADS, PK_TOPK * PK_TOPK)
        cand_i = (top_i[:, :, 0, :, None] * N_KEYS + top_i[:, :, 1, None, :]).reshape(tn, PEER_HEADS, PK_TOPK * PK_TOPK)
        best_s, best_j = lax.top_k(cand_s, PK_TOPK)
        experts = jnp.take_along_axis(cand_i, best_j, axis=-1)
        gates = jax.nn.softmax(best_s, axis=-1).astype(xb.dtype)
        act = jax.nn.gelu(jnp.einsum('thkd,td->thk', expert_u[experts], xb), approximate=False)
        return jnp.einsum('thk,thkd->td', gates * act, expert_v[experts])

    out = lax.map(block, xt.reshape(-1, PEER_BLOCK, D_MODEL))
    return out.reshape(n_pad, D_MODEL)[:n].reshape(shp)

def setup_inputs(seed: int = 0) -> dict:
    key = jax.random.key(seed)
    ks = jax.random.split(key, 32)
    f32 = jnp.float32
    n_pages = PAST_LEN // PAGE_SIZE
    n_pool = (5 * DEC_BATCH * n_pages + 3) // 4

    def nrm(k, shape, s=1.0):
        return s * jax.random.normal(k, shape, f32)

    x_prompt = nrm(ks[0], (BATCH, SEQ, D_MODEL))
    x_sample = nrm(ks[1], (DEC_BATCH, DEC_SEQ, D_MODEL))
    cache_k = nrm(ks[2], (DEPTH, n_pool, PAGE_SIZE, ATT_HEADS, ATT_HEAD_DIM))
    cache_v = nrm(ks[3], (DEPTH, n_pool, PAGE_SIZE, ATT_HEADS, ATT_HEAD_DIM))
    cache_logf = jax.nn.log_sigmoid(CACHE_FORGET_BIAS + nrm(ks[4], (DEPTH, n_pool, PAGE_SIZE, ATT_HEADS), 0.5))
    state_ssm = nrm(ks[5], (DEPTH, DEC_BATCH, SSM_HEADS, SSM_HEAD_DIM, SSM_STATE), 0.1)
    state_conv = nrm(ks[6], (DEPTH, DEC_BATCH, CONV_WIDTH - 1, CONV_DIM))
    page_table = jax.random.permutation(ks[7], n_pool)[: DEC_BATCH * n_pages].reshape(DEC_BATCH, n_pages).astype(jnp.int32)
    w_in = nrm(ks[8], (DEPTH, D_MODEL, N_IN), D_MODEL ** -0.5)
    b_fgate = jax.random.uniform(ks[9], (DEPTH, ATT_HEADS), f32, 1.0, 4.0)
    conv_w = nrm(ks[10], (DEPTH, CONV_WIDTH, CONV_DIM), CONV_WIDTH ** -0.5)
    conv_b = nrm(ks[11], (DEPTH, CONV_DIM), 0.01)
    dt0 = jnp.exp(jax.random.uniform(ks[12], (DEPTH, SSM_HEADS), f32, math.log(1e-3), math.log(1e-1)))
    dt_bias = dt0 + jnp.log(-jnp.expm1(-dt0))
    a_log = jnp.log(jax.random.uniform(ks[13], (DEPTH, SSM_HEADS), f32, 1.0, 16.0))
    d_skip = 1.0 + nrm(ks[14], (DEPTH, SSM_HEADS), 0.1)
    ssm_norm_w = 1.0 + nrm(ks[15], (DEPTH, D_SSM), 0.1)
    w_br_att = nrm(ks[16], (DEPTH, D_ATT, D_MODEL), D_ATT ** -0.5)
    w_br_ssm = nrm(ks[17], (DEPTH, D_SSM, D_MODEL), D_SSM ** -0.5)
    w_out = nrm(ks[18], (DEPTH, D_MODEL, D_MODEL), DEEPNORM_BETA * D_MODEL ** -0.5)
    ln1_g = 1.0 + nrm(ks[19], (DEPTH, D_MODEL), 0.1)
    ln1_b = nrm(ks[20], (DEPTH, D_MODEL), 0.01)
    w_query = nrm(ks[21], (DEPTH, D_MODEL, PEER_HEADS * PK_DIM), D_MODEL ** -0.5)
    sub_keys = nrm(ks[22], (DEPTH, PEER_HEADS, 2, N_KEYS, PK_HALF), PK_HALF ** -0.5)
    expert_u = nrm(ks[23], (DEPTH, N_EXPERTS, D_MODEL), D_MODEL ** -0.5)
    expert_v = nrm(ks[24], (DEPTH, N_EXPERTS, D_MODEL), DEEPNORM_BETA)
    ln2_g = 1.0 + nrm(ks[25], (DEPTH, D_MODEL), 0.1)
    ln2_b = nrm(ks[26], (DEPTH, D_MODEL), 0.01)
    return {'x_prompt': x_prompt, 'x_sample': x_sample, 'cache_k': cache_k, 'cache_v': cache_v,
            'cache_logf': cache_logf, 'state_ssm': state_ssm, 'state_conv': state_conv,
            'page_table': page_table, 'w_in': w_in, 'b_fgate': b_fgate, 'conv_w': conv_w,
            'conv_b': conv_b, 'dt_bias': dt_bias, 'a_log': a_log, 'd_skip': d_skip,
            'ssm_norm_w': ssm_norm_w, 'w_br_att': w_br_att, 'w_br_ssm': w_br_ssm, 'w_out': w_out,
            'ln1_g': ln1_g, 'ln1_b': ln1_b, 'w_query': w_query, 'sub_keys': sub_keys,
            'expert_u': expert_u, 'expert_v': expert_v, 'ln2_g': ln2_g, 'ln2_b': ln2_b}

def reference(x_prompt, x_sample, cache_k, cache_v, cache_logf, state_ssm, state_conv, page_table,
              w_in, b_fgate, conv_w, conv_b, dt_bias, a_log, d_skip, ssm_norm_w,
              w_br_att, w_br_ssm, w_out, ln1_g, ln1_b, w_query, sub_keys, expert_u, expert_v,
              ln2_g, ln2_b):
    n_seq = x_prompt.shape[0]
    dec_b = x_sample.shape[0]
    xp, xs = x_prompt, x_sample
    kp_l, vp_l, fp_l, hp_l, cp_l = [], [], [], [], []
    ks_l, vs_l, fs_l, hs_l, cs_l = [], [], [], [], []
    for i in range(DEPTH):
        ssm_w = (conv_w[i], conv_b[i], dt_bias[i], a_log[i], d_skip[i], ssm_norm_w[i])
        merge_w = (w_br_att[i], w_br_ssm[i], w_out[i], ln1_g[i], ln1_b[i])
        peer_w = (w_query[i], sub_keys[i], expert_u[i], expert_v[i])

        q, k, v, logf, z, xbc, dt_raw, ga, gs = mixer_inputs(xp, w_in[i], b_fgate[i])
        att = fox_prompt(q, k, v, logf)
        buf0 = jnp.zeros((n_seq, CONV_WIDTH - 1, CONV_DIM), xp.dtype)
        h0 = jnp.zeros((n_seq, SSM_HEADS, SSM_HEAD_DIM, SSM_STATE), jnp.float32)
        ssm, conv_new, h_new = mamba_branch(z, xbc, dt_raw, buf0, h0, *ssm_w)
        xp = merge_branches(xp, att, ssm, ga, gs, *merge_w)
        xp = layer_norm(DEEPNORM_ALPHA * xp + peer(xp, *peer_w), ln2_g[i], ln2_b[i])
        kp_l.append(k); vp_l.append(v); fp_l.append(logf); hp_l.append(h_new); cp_l.append(conv_new)

        q, k, v, logf, z, xbc, dt_raw, ga, gs = mixer_inputs(xs, w_in[i], b_fgate[i])
        k_past = cache_k[i][page_table].reshape(dec_b, -1, ATT_HEADS, ATT_HEAD_DIM)
        v_past = cache_v[i][page_table].reshape(dec_b, -1, ATT_HEADS, ATT_HEAD_DIM)
        f_past = cache_logf[i][page_table].reshape(dec_b, -1, ATT_HEADS)
        att = fox_sample(q, k, v, logf, k_past, v_past, f_past)
        ssm, conv_new, h_new = mamba_branch(z, xbc, dt_raw, state_conv[i], state_ssm[i], *ssm_w)
        xs = merge_branches(xs, att, ssm, ga, gs, *merge_w)
        xs = layer_norm(DEEPNORM_ALPHA * xs + peer(xs, *peer_w), ln2_g[i], ln2_b[i])
        ks_l.append(k); vs_l.append(v); fs_l.append(logf); hs_l.append(h_new); cs_l.append(conv_new)

    k_prompt = jnp.stack(kp_l)
    v_prompt = jnp.stack(vp_l)
    logf_prompt = jnp.stack(fp_l)
    ssm_prompt = jnp.stack(hp_l)
    conv_prompt = jnp.stack(cp_l)
    k_sample = jnp.stack(ks_l)
    v_sample = jnp.stack(vs_l)
    logf_sample = jnp.stack(fs_l)
    ssm_sample = jnp.stack(hs_l)
    conv_sample = jnp.stack(cs_l)
    return (xp, xs, k_prompt, v_prompt, logf_prompt, ssm_prompt, conv_prompt,
            k_sample, v_sample, logf_sample, ssm_sample, conv_sample)


_drawn_inputs = setup_inputs


def setup_inputs(seed=0):
    import zlib

    import numpy as np

    out = dict(_drawn_inputs(seed))
    spreads = {}
    factors = {'cache_logf': 165.627, 'conv_b': 3.328, 'ln2_b': 5.813}
    for name, (base, spread) in spreads.items():
        noise = np.random.default_rng([zlib.crc32(name.encode()), seed]).standard_normal(out[name].shape)
        drawn = base * np.exp(spread * noise) if base else spread * noise
        out[name] = __import__('jax').numpy.asarray(drawn.astype(out[name].dtype))
    for name, factor in factors.items():
        out[name] = (out[name] * factor).astype(out[name].dtype)
    return out
```

```python
from contextlib import ExitStack

import concourse.bass as bass
from concourse import mybir

F32 = mybir.dt.float32
F32R = mybir.dt.float32r
I32 = mybir.dt.int32
U32 = mybir.dt.uint32
ALU = mybir.AluOpType
ACT = mybir.ActivationFunctionType
AX = mybir.AxisListType.X
ds = bass.ds

P = 128
D = 2048
KT = D // P
TP, NB, TB = 512, 8, 8
TS = NB * TB
T = TP + TS
HALF = T // 2
AH, DH = 16, 64
DA = AH * DH
SH, SG, SR, SN = 32, 8, 4, 128
PAGES, PAGE = 16, 128
PH, NK, TOPK = 8, 128, 16
PICKS = PH * TOPK
ALPHA = 2.0 ** 0.25
EPS = 1e-5
NEG = -1e30
LOW = -3.0e38
Q0, K0, Z0, X0, B0, C0, GA0, GS0, MISC = 0, 8, 16, 32, 48, 56, 64, 80, 96
NT = 97
TT = [(i * P, min(P, T - i * P)) for i in range(5)]


class Tools:

    def __init__(self, nc, ctx):
        self.nc, self.whole = nc, ctx

    def pool_sem(self, name):
        return self.whole.enter_context(self.nc.semaphore(name))

    def sem(self, name):
        self.sems.append(self.ctx.enter_context(self.nc.semaphore(name)))
        return self.sems[-1]

    def run(self, stage, *args):
        self.sems, self.held = [], {}
        with ExitStack() as self.ctx:
            stage(self.nc, self, *args)
            with self.nc.Block() as block:
                @block.gpsimd
                def _(pool):
                    for s in self.sems:
                        pool.sem_clear(s)

    def hold(self, eng, name):
        if name not in self.held:
            self.held[name] = self.sem("held_" + name)
        eng.sem_inc(self.held[name], 1)


def diagonal(ap, rows, width, blocks, start, size):
    v = ap.rearrange("p (j c) -> p j c", c=width + 2 * size)
    return v[rows[0]:rows[1], 0:blocks, start:start + size]


def project_in(nc, tl, io, dr):
    RING = 4
    V_BLOCKS = KT // 4
    V_ITEMS = 2 * V_BLOCKS
    ITEMS = NT + V_ITEMS
    VT = [(t0 if n == P else T - P, P - n) for t0, n in TT]
    with ExitStack() as ctx:
        sb = lambda n, s, d=F32: ctx.enter_context(nc.sbuf_tensor(n, s, d))
        xh = sb("a_xh", [P, KT, T], F32R)
        xl = sb("a_xl", [P, KT, T], F32R)
        w = sb("a_w", [P, RING, KT * P])
        wh = sb("a_wh", [P, 2, KT * P], F32R)
        wl = sb("a_wl", [P, 2, KT * P], F32R)
        out = sb("a_out", [P, RING, T])
        vout = sb("a_vout", [P, 2, 5, 512])
        acc = ctx.enter_context(nc.psum_tensor("a_acc", [P, 8, 512], F32))
        x_in = [tl.sem(f"a_x_in{q}") for q in range(4)]
        xh_out = tl.sem("a_xh_out")
        xl_out = tl.sem("a_xl_out")
        w_in = [tl.sem(f"a_w_in{s}") for s in range(RING)]
        wh_out = tl.sem("a_wh_out")
        w_split = tl.sem("a_w_split")
        tile_done = tl.sem("a_tile_done")
        copied_a = tl.sem("a_copied_a")
        copied_v = tl.sem("a_copied_v")
        flight = tl.pool_sem("a_flight")
        stored = [tl.sem(f"a_stored{s}") for s in range(RING)]
        v_copied_a = tl.sem("a_v_copied_a")
        v_copied_v = tl.sem("a_v_copied_v")
        v_stored = tl.sem("a_v_stored")
        rounds, rest = divmod(NT, RING)
        flat = lambda buf: buf.rearrange("p a b -> p (a b)")[:, 0:4 * T]
        stage = [flat(out[:, :, :]), flat(vout[:, 0, :, :]), flat(vout[:, 1, :, :]), flat(out[:, :, :])]
        quarter = lambda x, q: x[:, 4 * q:4 * q + 4, :].rearrange("p k n -> p (k n)")

        def every_tile(eng, body):
            with eng.Fori(0, rounds) as r:
                for s in range(RING):
                    body(r, s)
            for s in range(rest):
                body(rounds, s)

        def split_waits(eng, m):
            r, s = m
            eng.wait_ge(w_in[s], 16 * r + 16)
            eng.wait_ge(tile_done, RING * r + s + RING - 1)

        after = lambda r, s: (r, s + 1) if s + 1 < RING else (r + 1, 0)
        item = lambda m: (m // RING, m % RING)

        def converter(eng, split, copy, v_copy):
            split(item(0))

            def body(r, s):
                split(after(r, s))
                copy(r, s)
            every_tile(eng, body)
            for m in range(NT + 1, ITEMS):
                split(item(m))
                if m == NT + V_BLOCKS + 1:
                    v_copy(0)
            v_copy(1)

        with nc.Block() as block:
            @block.sync
            def _(sp):
                for q in range(3):
                    sp.dma_start(stage[q], io["xT"][:, 4 * q:4 * q + 4, :].rearrange("p k n -> p (k n)")).then_inc(x_in[q], 16)
                sp.dma_start(w[:, 0, :], io["w_in"][0].rearrange("p k n -> p (k n)")).then_inc(w_in[0], 16)
                sp.wait_ge(xl_out, 1)
                sp.dma_start(stage[3], io["xT"][:, 12:16, :].rearrange("p k n -> p (k n)")).then_inc(x_in[3], 16)
                for s in range(1, RING):
                    sp.dma_start(w[:, s, :], io["w_in"][s].rearrange("p k n -> p (k n)")).then_inc(w_in[s], 16)

                def load(r, s):
                    sp.wait_ge(w_split, RING * (r - 1) + s + 1)
                    sp.dma_start(w[:, s, :], io["w_in"][ds(RING * r + s, 1)].rearrange("a p k n -> (a p) (k n)")
                                 ).then_inc(w_in[s], 16)
                with sp.Fori(1, rounds) as r:
                    for s in range(RING):
                        load(r, s)
                for s in range(rest):
                    load(rounds, s)
                for m in range(NT, ITEMS):
                    b, q = divmod(m - NT, V_BLOCKS)
                    sp.wait_ge(w_split, m - RING + 1)
                    sp.dma_start(w[:, m % RING, :], io["w_v"][b, :, 4 * q:4 * q + 4, :].rearrange("p k n -> p (k n)")
                                 ).then_inc(w_in[m % RING], 16)
                for b in range(2):
                    for i, (t0, skip) in enumerate(VT):
                        sp.wait_ge((v_copied_a, v_copied_v)[i % 2], (3, 2)[i % 2] * b + i // 2 + 1)
                        sp.dma_start(dr["v_tok"][t0 + skip:t0 + P, b * 512:b * 512 + 512], vout[skip:P, b, i, :]
                                     ).then_inc(v_stored, 16)
                sp.wait_ge(v_stored, 160)

            @block.tensor
            def _(pe):
                pe.sem_inc(tile_done, RING)
                pe.wait_ge(xl_out, 4)

                def product(r, s):
                    pe.wait_ge(w_split, RING * r + s + 1)
                    pe.wait_ge(copied_a, RING * r + s + 1)
                    pe.wait_ge(copied_v, RING * r + s + 1)
                    for k in range(KT):
                        for weights, x in ((wh, xh), (wh, xl), (wl, xh)):
                            for h in range(2):
                                last = nc.tensor.matmul(acc[:, 2 * s + h, 0:HALF], weights[:, s % 2, k * P:(k + 1) * P],
                                                        x[:, k, h * HALF:(h + 1) * HALF],
                                                        start=(k == 0 and x is xh and weights is wh),
                                                        stop=(k == KT - 1 and weights is wl))
                    last.then_inc(tile_done, 1)
                every_tile(pe, product)
                for b in range(2):
                    pe.wait_ge(copied_a, NT - 1 + b + RING)
                    pe.wait_ge(copied_v, NT - 1 + b + RING)
                    for q in range(V_BLOCKS):
                        m = NT + b * V_BLOCKS + q
                        pe.wait_ge(w_split, m + 1)
                        for i, (t0, _) in enumerate(VT):
                            if b == 1 and q == 0 and i >= 3:
                                pe.wait_ge((v_copied_a, v_copied_v)[i - 3], 1)
                            for k in range(4):
                                for x, weights in ((xh, wh), (xl, wh), (xh, wl)):
                                    last = nc.tensor.matmul(acc[:, (2 + 5 * b + i) % 8, :], x[:, 4 * q + k, t0:t0 + P],
                                                            weights[:, m % 2, k * 512:(k + 1) * 512],
                                                            start=(q == 0 and k == 0 and x is xh and weights is wh),
                                                            stop=(q == V_BLOCKS - 1 and k == 3 and weights is wl))
                        last.then_inc(tile_done, 1)

            @block.scalar
            def _(act):
                act.sem_inc(copied_a, RING)
                for q in range(4):
                    act.wait_ge(x_in[q], 16)
                    nc.scalar.copy(quarter(xh, q), stage[q]).then_inc(xh_out, 1)

                def split(m):
                    split_waits(act, m)
                    nc.scalar.copy(wh[:, m[1] % 2, :], w[:, m[1], :]).then_inc(wh_out, 1)

                def copy(r, s):
                    act.wait_ge(tile_done, RING * r + s + 1 + RING)
                    act.wait_ge(stored[s], 16 * r + 16)
                    nc.scalar.copy(out[:, s, 0:HALF], acc[:, 2 * s, 0:HALF]).then_inc(copied_a, 1)

                def v_copy(b):
                    act.wait_ge(tile_done, NT + (b + 1) * V_BLOCKS + RING)
                    for i in range(0, 5, 2):
                        nc.scalar.copy(vout[:, b, i, :], acc[:, (2 + 5 * b + i) % 8, :]).then_inc(v_copied_a, 1)
                converter(act, split, copy, v_copy)

            @block.vector
            def _(dve):
                dve.sem_inc(copied_v, RING)
                for q in range(4):
                    dve.wait_ge(xh_out, q + 1)
                    nc.vector.tensor_tensor(quarter(xl, q), stage[q], quarter(xh, q), ALU.subtract).then_inc(xl_out, 1)

                def split(m):
                    r, s = m
                    dve.wait_ge(wh_out, RING * r + s + 1)
                    nc.vector.tensor_tensor(wl[:, s % 2, :], w[:, s, :], wh[:, s % 2, :], ALU.subtract).then_inc(w_split, 1)

                def copy(r, s):
                    dve.wait_ge(tile_done, RING * r + s + 1 + RING)
                    dve.wait_ge(stored[s], 16 * r + 16)
                    nc.vector.tensor_copy(out[:, s, HALF:T], acc[:, 2 * s + 1, 0:HALF]).then_inc(copied_v, 1)

                def v_copy(b):
                    dve.wait_ge(tile_done, NT + (b + 1) * V_BLOCKS + RING)
                    for i in range(1, 5, 2):
                        nc.vector.tensor_copy(vout[:, b, i, :], acc[:, (2 + 5 * b + i) % 8, :]).then_inc(v_copied_v, 1)
                converter(dve, split, copy, v_copy)

            @block.gpsimd
            def _(pool):
                for s in range(RING):
                    pool.sem_inc(stored[s], 16)

                def store(r, s):
                    pool.wait_ge(copied_a, RING * r + s + 1 + RING)
                    pool.wait_ge(copied_v, RING * r + s + 1 + RING)
                    tl.hold(pool, "a_pool")
                    pool.dma_start(dr["uT"][ds(RING * r + s, 1)].rearrange("a p n -> (a p) n"), out[:, s, :]
                                   ).then_inc(flight, 16)
                    pool.wait_ge(flight, 16 * (RING * r + s) + 16)
                    pool.sem_inc(stored[s], 16)
                every_tile(pool, store)


def gate_scalars(nc, tl, io, dr):
    with ExitStack() as ctx:
        sb = lambda n, s: ctx.enter_context(nc.sbuf_tensor(n, s, F32))
        m = sb("b_m", [64, T])
        e = sb("b_e", [64, T])
        u = sb("b_u", [64, T])
        l = sb("b_l", [64, T])
        c = sb("b_c", [64, T])
        cum = sb("b_cum", [64, T])
        ncum = sb("b_ncum", [AH, T])
        reset = sb("b_reset", [64, T])
        par = sb("b_par", [64, 2])
        na = sb("b_na", [64, 1])
        w = sb("b_w", [64, T])
        fac = sb("b_fac", [96, T])
        facg = sb("b_facg", [P, SG, 5, 3, SR])
        ident = sb("b_ident", [P, P])
        ps = ctx.enter_context(nc.psum_tensor("b_ps", [P, 5, 512], F32))
        loaded = tl.sem("b_loaded")
        a_done = tl.sem("b_a_done")
        v_done = tl.sem("b_v_done")
        turned = tl.sem("b_turned")
        stored = tl.sem("b_stored")
        with nc.Block() as block:
            @block.sync
            def _(sp):
                sp.dma_start(m[:, :], dr["uT"][MISC, 0:64, :]).then_inc(loaded, 16)
                sp.dma_start(par[:, :], io["gate_par"]).then_inc(loaded, 16)
                sp.dma_start(reset[:, :], io["reset"]).then_inc(loaded, 16)
                sp.dma_start(ident[:, :], io["ident"]).then_inc(loaded, 16)
                sp.dma_start(dr["kT_out"], dr["uT"][K0:K0 + 8]).then_inc(stored, 16)
                sp.wait_ge(v_done, 5)
                sp.dma_start(dr["logfT"], l[0:AH, :]).then_inc(stored, 16)
                sp.dma_start(dr["cum"], cum[0:AH, :]).then_inc(stored, 16)
                sp.dma_start(dr["ncum"], ncum[:, :]).then_inc(stored, 16)
                sp.dma_start(dr["cs"], cum[32:64, :]).then_inc(stored, 16)
                sp.wait_ge(v_done, 8)
                sp.dma_start(dr["facg"].rearrange("g p n -> p g n"),
                             facg[:, :, :, :, :].rearrange("p g a q r -> p g (a q r)")).then_inc(stored, 16)
                sp.wait_ge(stored, 96)

            @block.scalar
            def _(act):
                act.wait_ge(loaded, 64)
                nc.scalar.activation(na[32:64, :], par[32:64, 1:2], ACT.Exp).then_inc(a_done, 1)
                act.wait_ge(v_done, 1)
                nc.scalar.activation(e[:, :], c[:, :], ACT.Exp, scale=-1.0).then_inc(a_done, 1)
                act.wait_ge(v_done, 2)
                nc.scalar.activation(l[:, :], u[:, :], ACT.Ln).then_inc(a_done, 1)
                act.wait_ge(v_done, 6)
                nc.scalar.activation(w[32:64, :], w[32:64, :], ACT.Exp).then_inc(a_done, 1)

            @block.vector
            def _(dve):
                v = nc.vector
                dve.wait_ge(loaded, 64)
                v.tensor_scalar(m[:, :], m[:, :], par[:, 0:1], None, ALU.add)
                dve.drain()
                v.scalar_tensor_tensor(c[:, :], m[:, :], -1.0, m[:, :], ALU.mult, ALU.max).then_inc(v_done, 1)
                dve.wait_ge(a_done, 2)
                v.tensor_scalar(u[:, :], e[:, :], 1.0, None, ALU.add).then_inc(v_done, 1)
                dve.drain()
                v.scalar_tensor_tensor(c[:, :], u[:, :], -1.0, e[:, :], ALU.add, ALU.subtract)
                dve.wait_ge(a_done, 3)
                v.reciprocal(u[:, :], u[:, :])
                dve.drain()
                v.tensor_tensor(c[:, :], c[:, :], u[:, :], ALU.mult)
                dve.drain()
                v.tensor_tensor(l[:, :], l[:, :], c[:, :], ALU.subtract)
                dve.drain()
                v.scalar_tensor_tensor(l[0:32, :], m[0:32, :], 0.0, l[0:32, :], ALU.min, ALU.subtract)
                v.scalar_tensor_tensor(m[32:64, :], m[32:64, :], 0.0, l[32:64, :], ALU.max, ALU.add)
                dve.drain()
                v.tensor_scalar(na[32:64, :], na[32:64, :], -1.0, None, ALU.mult)
                v.tensor_tensor_scan(cum[0:32, :], reset[0:32, :], l[0:32, :], 0.0, ALU.mult, ALU.add)
                dve.drain()
                v.tensor_scalar(ncum[:, :], cum[0:AH, :], -1.0, None, ALU.mult).then_inc(v_done, 1)
                v.tensor_scalar(c[32:64, :], m[32:64, :], na[32:64, :], None, ALU.mult)
                dve.drain().then_inc(v_done, 1)
                v.tensor_tensor_scan(cum[32:64, :], reset[32:64, :], c[32:64, :], 0.0, ALU.mult, ALU.add)
                dve.drain().then_inc(v_done, 1)
                for a, b, n in ((0, TP, P), (TP, T, TB)):
                    cv = cum[32:64, a:b].rearrange("p (c t) -> p c t", t=n)
                    last = v.tensor_tensor(w[32:64, a:b].rearrange("p (c t) -> p c t", t=n),
                                           cv[:, :, n - 1:n].to_broadcast([32, (b - a) // n, n]), cv, ALU.subtract)
                last.then_inc(v_done, 1)
                v.tensor_copy(fac[0:32, :], m[32:64, :])
                v.tensor_copy(fac[32:64, :], cum[32:64, :])
                dve.wait_ge(a_done, 4)
                v.tensor_tensor(w[32:64, :], w[32:64, :], m[32:64, :], ALU.mult)
                dve.drain()
                v.tensor_copy(fac[64:96, :], w[32:64, :]).then_inc(v_done, 1)
                dve.wait_ge(turned, 5)
                for i, (t0, n) in enumerate(TT):
                    last = v.tensor_copy(facg[0:n, :, i, :, :].rearrange("p g q r -> p q g r"),
                                         ps[0:n, i, 0:96].rearrange("p (q g r) -> p q g r", q=3, g=SG))
                if TT[4][1] < P:
                    last = v.memset(facg[TT[4][1]:P, :, 4, :, :], 0.0)
                last.then_inc(v_done, 1)

            @block.tensor
            def _(pe):
                pe.wait_ge(v_done, 7)
                for i, (t0, n) in enumerate(TT):
                    nc.tensor.transpose(ps[0:n, i, 0:96], fac[:, t0:t0 + n], ident[0:96, 0:96]).then_inc(turned, 1)


def mamba(nc, tl, io, dr):
    FACN = 5 * 3 * SR
    GC = 24
    with ExitStack() as ctx:
        sb = lambda n, s: ctx.enter_context(nc.sbuf_tensor(n, s, F32))
        pb = lambda n, s: ctx.enter_context(nc.psum_tensor(n, s, F32))
        raw = sb("c_raw", [P, 2, 4, T])
        old = sb("c_old", [P, 2, 4, NB, 3])
        gc = sb("c_gc", [P, 2, GC])
        tf = sb("c_tf", [P, 2, FACN])
        z = sb("c_z", [P, 2, 2, T])
        csb = sb("c_csb", [P, 2, SR, T])
        csj = sb("c_csj", [P, 2, 2, T])
        h0 = sb("c_h0", [P, 2, NB, 2 * P])
        samp = sb("c_samp", [P, 4, NB, 3 + TB])
        xc = sb("c_xc", [P, 4, T])
        tail = sb("c_tail", [P, 4, 3 + NB * 3])
        xpad = sb("c_xpad", [P, SR, P])
        xst = sb("c_xst", [P, 2 * P])
        btok = sb("c_btok", [P, P])
        bmask = sb("c_bmask", [P, NB, P])
        seg = sb("c_seg", [P, SR, P])
        mm = sb("c_mm", [P, SR, P])
        cd = sb("c_cd", [P, SR, 4 + NB])
        hT = sb("c_hT", [P, 2 * P])
        hs = sb("c_hs", [P, NB, 2 * P])
        y = sb("c_y", [P, 2, T])
        t2 = sb("c_t2", [P, 2, P])
        sq = sb("c_sq", [P, 2, T])
        ms = sb("c_ms", [P, T])
        mo = sb("c_mo", [P, 2, T])
        ident = sb("c_ident", [P, P])
        mask_p = sb("c_mask_p", [P, P])
        mask_s = sb("c_mask_s", [TS, TS])
        seqm = sb("c_seqm", [TS, NB])
        ones = sb("c_ones", [P, P])
        p_tok = pb("c_p_tok", [P, 2, 512])
        p_cb = pb("c_p_cb", [P, 512])
        p_y = pb("c_p_y", [P, 2, 2 * P])
        p_o = pb("c_p_o", [P, 2, 2 * P])
        p_s = pb("c_p_s", [P, 2, 512])
        p_n = pb("c_p_n", [P, 512])
        const_in = tl.sem("c_const_in")
        loaded = [tl.sem(f"c_loaded{k}") for k in range(2)]
        group_done = tl.sem("c_group_done")
        padded = tl.sem("c_padded")
        conv_sum = tl.sem("c_conv_sum")
        conv_out = tl.sem("c_conv_out")
        exp_out = tl.sem("c_exp_out")
        tok_out = tl.sem("c_tok_out")
        tok_free = tl.sem("c_tok_free")
        b_out = tl.sem("c_b_out")
        seg_out = tl.sem("c_seg_out")
        decay_out = tl.sem("c_decay_out")
        m_out = tl.sem("c_m_out")
        y_out = tl.sem("c_y_out")
        h_out = tl.sem("c_h_out")
        bm_out = tl.sem("c_bm_out")
        s_out = tl.sem("c_s_out")
        s_free = tl.sem("c_s_free")
        sq_out = tl.sem("c_sq_out")
        n_out = tl.sem("c_n_out")
        n_free = tl.sem("c_n_free")
        root_out = tl.sem("c_root_out")
        flight = tl.pool_sem("c_flight")
        st = [tl.sem(f"c_stored{i}") for i in range(4)]
        CH = [(i * P, P) for i in range(4)] + [(TP, TS)]

        def groups(eng, body):
            with eng.Fori(0, SG // 2) as r:
                for k in range(2):
                    body(2 * r + k, r, k)

        with nc.Block() as block:
            @block.sync
            def _(sp):
                for dst, src in ((ident, "ident"), (mask_p, "mask_st"), (mask_s, "mask_ss"), (seqm, "seqm"), (ones, "ones")):
                    sp.dma_start(dst[:, :], io[src]).then_inc(const_in, 16)

                def load(g, r, k):
                    sp.wait_ge(group_done, g + 1)
                    sp.dma_start(raw[:, k, 0:2, :], dr["uT"][ds(2 * g + X0, 2)].rearrange("a p n -> p a n")).then_inc(loaded[k], 16)
                    for j, t0 in ((2, B0), (3, C0)):
                        sp.dma_start(raw[:, k, j, :], dr["uT"][ds(g + t0, 1)].rearrange("a p n -> (a p) n")).then_inc(loaded[k], 16)
                    sp.dma_start(z[:, k, :, :], dr["uT"][ds(2 * g + Z0, 2)].rearrange("a p n -> p a n")).then_inc(loaded[k], 16)
                    sp.dma_start(old[:, k, :, :, :].rearrange("p a b c -> p (a b c)"),
                                 io["conv_old"][ds(g, 1)].rearrange("a p n -> (a p) n")).then_inc(loaded[k], 16)
                    sp.dma_start(gc[:, k, :], io["group_par"][ds(g, 1)].rearrange("a p n -> (a p) n")).then_inc(loaded[k], 16)
                    sp.dma_start(tf[:, k, :], dr["facg"][ds(g, 1)].rearrange("a p n -> (a p) n")).then_inc(loaded[k], 16)
                    for q in range(SR):
                        sp.dma_start(csb[:, k, q, :], dr["cs"][ds(SR * g + q, 1), :].to_broadcast([P, T])).then_inc(loaded[k], 16)
                        sp.dma_start(csj[64 * (q % 2):64 * (q % 2) + 64, k, q // 2, :],
                                     dr["cs"][ds(SR * g + q, 1), :].to_broadcast([64, T])).then_inc(loaded[k], 16)
                    sp.dma_start(h0[:, k, :, :], io["ssm_old"][ds(g, 1)].rearrange("a p b n -> (a p) b n")).then_inc(loaded[k], 16)
                groups(sp, load)
            NLOAD = 16 * (1 + 2 + 1 + 1 + 1 + 1 + 8 + 1)

            @block.vector
            def _(dve):
                v = nc.vector
                dve.wait_ge(const_in, 80)
                dve.sem_inc(group_done, 2)
                dve.sem_inc(tok_free, 2)
                dve.sem_inc(h_out, 1)
                dve.sem_inc(s_free, 2)
                dve.sem_inc(n_free, 1)
                v.memset(xpad[:, :, :], 0.0)

                def group(g, r, k):
                    dve.wait_ge(loaded[k], NLOAD * r + NLOAD)
                    dve.wait_ge(st[0], 16 * g + 16)
                    for a in range(4):
                        v.tensor_copy(samp[:, a, :, 0:3], old[:, k, a, :, :])
                        v.tensor_copy(samp[:, a, :, 3:3 + TB], raw[:, k, a, TP:T].rearrange("p (b t) -> p b t", t=TB))
                        v.tensor_copy(tail[:, a, 0:3], raw[:, k, a, TP - 3:TP])
                    dve.drain()
                    for a in range(4):
                        last = v.tensor_copy(tail[:, a, 3:3 + 3 * NB].rearrange("p (b c) -> p b c", c=3), samp[:, a, :, TB:TB + 3])
                    last.then_inc(padded, 1)
                    for a in range(4):
                        tap = lambda j: gc[:, k, 4 * a + j:4 * a + j + 1]
                        sv = xc[:, a, TP:T].rearrange("p (b t) -> p b t", t=TB)
                        v.tensor_scalar(xc[:, a, 0:TP], raw[:, k, a, 0:TP], tap(3), gc[:, k, 16 + a:17 + a], ALU.mult, ALU.add)
                        v.tensor_scalar(sv, samp[:, a, :, 3:3 + TB], tap(3), gc[:, k, 16 + a:17 + a], ALU.mult, ALU.add)
                        for j in range(3):
                            s = 3 - j
                            dve.drain()
                            v.scalar_tensor_tensor(xc[:, a, s:TP], raw[:, k, a, 0:TP - s], tap(j), xc[:, a, s:TP], ALU.mult, ALU.add)
                            last = v.scalar_tensor_tensor(sv, samp[:, a, :, j:j + TB], tap(j), sv, ALU.mult, ALU.add)
                        last.then_inc(conv_sum, 1)
                    dve.wait_ge(exp_out, g + 1)
                    dve.wait_ge(st[2], 16 * g + 16)
                    dve.wait_ge(st[3], 16 * g + 16)
                    for c, (t0, n) in enumerate(CH):
                        ck = 5 * g + c
                        fac = lambda q, i: tf[0:n, k, c * 12 + q * SR + i:c * 12 + q * SR + i + 1]
                        slot = (k * 5 + c) % 2
                        dve.wait_ge(tok_out, ck + 1)
                        for i in range(SR):
                            xin = p_tok[0:n, slot, 64 * i:64 * i + 64]
                            v.tensor_scalar(xpad[0:n, i, 64 * (i % 2):64 * (i % 2) + 64], xin, fac(0, i), None, ALU.mult)
                            v.tensor_scalar(xst[0:n, 64 * i:64 * i + 64], xin, fac(2, i), None, ALU.mult)
                        v.tensor_copy(btok[0:n, :], p_tok[0:n, slot, 256:384]).then_inc(b_out, 1)
                        for i in range(SR):
                            last = v.scalar_tensor_tensor(seg[0:n, i, 0:n], csb[0:n, k, i, t0:t0 + n], fac(1, i),
                                                          (mask_p if n == P else mask_s)[0:n, 0:n], ALU.subtract, ALU.add)
                        last.then_inc(seg_out, 1)
                        if c == 4:
                            dve.drain()
                            for b in range(NB):
                                last = v.tensor_scalar(bmask[0:TS, b, :], btok[0:TS, :], seqm[:, b:b + 1], None, ALU.mult)
                            last.then_inc(bm_out, 1)
                        dve.wait_ge(decay_out, ck + 1)
                        cb = p_cb[0:n, 0:n].unsqueeze(1).to_broadcast([n, SR, n])
                        v.tensor_tensor(mm[0:n, :, 0:n], seg[0:n, :, 0:n], cb, ALU.mult).then_inc(m_out, 1)
                        dve.drain().then_inc(tok_free, 1)
                        dve.wait_ge(y_out, ck + 2)
                        if c > 0:
                            v.tensor_tensor(t2[:, :, 0:n], p_o[:, :, 0:n], csj[:, k, :, t0:t0 + n], ALU.mult)
                            dve.drain()
                            v.tensor_tensor(t2[:, :, 0:n], p_y[:, :, 0:n], t2[:, :, 0:n], ALU.add)
                            dve.drain()
                        for j in range(2):
                            v.scalar_tensor_tensor(y[:, j, t0:t0 + n], xc[:, j, t0:t0 + n], gc[:, k, 20 + j:21 + j],
                                                   (p_y if c == 0 else t2)[:, j, 0:n], ALU.mult, ALU.add)
                        if c == 0:
                            v.tensor_copy(hT[:, :], p_s[:, 0, 0:2 * P])
                        elif c < 4:
                            for i in range(SR):
                                cols = slice(64 * i, 64 * i + 64)
                                v.scalar_tensor_tensor(hT[:, cols], hT[:, cols], cd[:, i, c:c + 1], p_s[:, 0, cols], ALU.mult, ALU.add)
                        dve.drain().then_inc(h_out, 1)
                    for u in range(NB // 2):
                        dve.wait_ge(s_out, 4 * g + u + 1)
                        for b in (2 * u, 2 * u + 1):
                            for i in range(SR):
                                cols = slice(64 * i, 64 * i + 64)
                                v.scalar_tensor_tensor(hs[:, b, cols], h0[:, k, b, cols], cd[:, i, 4 + b:5 + b],
                                                       p_s[:, u % 2, (b % 2) * 256 + 64 * i:(b % 2) * 256 + 64 * i + 64],
                                                       ALU.mult, ALU.add)
                        dve.drain().then_inc(s_free, 1)
                    v.tensor_tensor(y[:, :, :], y[:, :, :], z[:, k, :, :], ALU.mult)
                    dve.drain()
                    v.tensor_tensor(sq[:, :, :], y[:, :, :], y[:, :, :], ALU.mult).then_inc(sq_out, 1)
                    for h in range(2):
                        dve.wait_ge(n_out, 2 * g + h + 1)
                        v.tensor_scalar(ms[:, h * HALF:(h + 1) * HALF], p_n[:, 0:HALF], 1.0 / (2 * P), EPS, ALU.mult, ALU.add
                                        ).then_inc(n_free, 1)
                    dve.wait_ge(root_out, g + 1)
                    v.reciprocal(ms[:, :], ms[:, :])
                    dve.drain()
                    dve.wait_ge(st[1], 16 * g + 16)
                    for j in range(2):
                        v.scalar_tensor_tensor(mo[:, j, :], y[:, j, :], gc[:, k, 22 + j:23 + j], ms[:, :], ALU.mult, ALU.mult)
                    dve.drain().then_inc(group_done, 1)
                groups(dve, group)

            @block.scalar
            def _(act):
                def group(g, r, k):
                    act.wait_ge(loaded[k], NLOAD * r + NLOAD)
                    act.wait_ge(group_done, g + 2)
                    nc.scalar.activation(z[:, k, :, :], z[:, k, :, :], ACT.Silu)
                    for a in range(4):
                        act.wait_ge(conv_sum, 4 * g + a + 1)
                        nc.scalar.activation(xc[:, a, :], xc[:, a, :], ACT.Silu).then_inc(conv_out, 1)
                    nc.scalar.activation(csj[:, k, :, :], csj[:, k, :, :], ACT.Exp)
                    nc.scalar.activation(cd[:, :, 0:4], csb[:, k, :, P - 1:TP:P], ACT.Exp)
                    nc.scalar.activation(cd[:, :, 4:4 + NB], csb[:, k, :, TP + TB - 1:T:TB], ACT.Exp)
                    act.drain().then_inc(exp_out, 1)
                    for c, (t0, n) in enumerate(CH):
                        ck = 5 * g + c
                        act.wait_ge(seg_out, ck + 1)
                        nc.scalar.activation(seg[0:n, :, 0:n], seg[0:n, :, 0:n], ACT.Exp).then_inc(decay_out, 1)
                    act.wait_ge(n_free, 2 * g + 3)
                    nc.scalar.activation(ms[:, :], ms[:, :], ACT.Sqrt).then_inc(root_out, 1)
                groups(act, group)

            @block.tensor
            def _(pe):
                pe.wait_ge(const_in, 80)

                def group(g, r, k):
                    pe.wait_ge(loaded[k], NLOAD * r + NLOAD)
                    pe.wait_ge(conv_out, 4 * g + 4)
                    for c, (t0, n) in enumerate(CH):
                        ck = 5 * g + c
                        slot = (k * 5 + c) % 2
                        pe.wait_ge(tok_free, ck + 1)
                        if n < P:
                            tl.hold(pe, "c_pe")
                        for a in range(3):
                            nc.tensor.transpose(p_tok[0:n, slot, a * P:(a + 1) * P], xc[:, a, t0:t0 + n], ident[:, :])
                        pe.wait_ge(tok_free, ck + 2)
                        nc.tensor.matmul(p_cb[0:n, 0:n], xc[:, 2, t0:t0 + n], xc[:, 3, t0:t0 + n], start=True, stop=True
                                         ).then_inc(tok_out, 1)
                        pe.wait_ge(m_out, ck + 1)
                        pe.wait_ge(h_out, ck + 1)
                        for j in range(2):
                            for i in range(2):
                                nc.tensor.matmul(p_y[:, j, 0:n], xpad[0:n, 2 * j + i, :], mm[0:n, 2 * j + i, 0:n],
                                                 start=(i == 0), stop=(i == 1))
                        pe.wait_ge(b_out, ck + 1)
                        if c == 4:
                            for j in range(2):
                                for b in range(NB):
                                    last = nc.tensor.matmul(p_o[:, j, TB * b:TB * b + TB], h0[:, k, b, j * P:(j + 1) * P],
                                                            xc[:, 3, TP + TB * b:TP + TB * b + TB], start=True, stop=True)
                        else:
                            if c > 0:
                                for j in range(2):
                                    nc.tensor.matmul(p_o[:, j, 0:n], hT[:, j * P:(j + 1) * P], xc[:, 3, t0:t0 + n], start=True, stop=True)
                            last = nc.tensor.matmul(p_s[:, 0, 0:2 * P], btok[:, :], xst[:, :], start=True, stop=True)
                        last.then_inc(y_out, 1)
                    pe.wait_ge(bm_out, g + 1)
                    pe.wait_ge(h_out, 5 * g + 5)
                    for u in range(NB // 2):
                        pe.wait_ge(s_free, 4 * g + u + 1)
                        for b in (2 * u, 2 * u + 1):
                            last = nc.tensor.matmul(p_s[:, u % 2, (b % 2) * 256:(b % 2) * 256 + 256], bmask[0:TS, b, :], xst[0:TS, :],
                                                    start=True, stop=True)
                        last.then_inc(s_out, 1)
                    pe.wait_ge(sq_out, g + 1)
                    for h in range(2):
                        pe.wait_ge(n_free, 2 * g + h + 1)
                        for j in range(2):
                            last = nc.tensor.matmul(p_n[:, 0:HALF], ones[:, :], sq[:, j, h * HALF:(h + 1) * HALF],
                                                    start=(j == 0), stop=(j == 1))
                        last.then_inc(n_out, 1)
                pe.sem_inc(y_out, 1)
                groups(pe, group)

            @block.gpsimd
            def _(pool):
                for x in st:
                    pool.sem_inc(x, 16)

                def store(g, r, k):
                    pool.wait_ge(padded, g + 1)
                    tl.hold(pool, "c_pool")
                    pool.dma_start(dr["convT"][ds(g, 1)].rearrange("a p n -> (a p) n"),
                                   tail[:, :, :].rearrange("p a n -> p (a n)")).then_inc(flight, 16)
                    pool.wait_ge(flight, 64 * g + 16)
                    pool.sem_inc(st[0], 16)
                    pool.wait_ge(group_done, g + 3)
                    tl.hold(pool, "c_pool")
                    pool.dma_start(dr["mT"][ds(2 * g, 2)].rearrange("a p n -> p a n"), mo[:, :, :]).then_inc(flight, 16)
                    pool.dma_start(dr["ssm_pT"][ds(g, 1)].rearrange("a p n -> (a p) n"), hT[:, :]).then_inc(flight, 16)
                    pool.dma_start(dr["ssm_sT"][ds(g, 1)].rearrange("a p b n -> (a p) b n"), hs[:, :, :]).then_inc(flight, 16)
                    pool.wait_ge(flight, 64 * g + 64)
                    for x in st[1:]:
                        pool.sem_inc(x, 16)
                groups(pool, store)


def prompt_attention(nc, tl, io, dr):
    QB = TP // P
    KA = DH + 2
    with ExitStack() as ctx:
        sb = lambda n, s: ctx.enter_context(nc.sbuf_tensor(n, s, F32))
        pb = lambda n, s: ctx.enter_context(nc.psum_tensor(n, s, F32))
        qraw = sb("d_qraw", [DH, 2, TP])
        qa = sb("d_qa", [KA, 2, TP])
        ka = sb("d_ka", [KA, 2, TP])
        vv = sb("d_v", [P, 2, QB, DH])
        pr = sb("d_pr", [P, 2, TP])
        pT = sb("d_pT", [P, 2, QB, P])
        mx = sb("d_mx", [P, 2])
        nm = sb("d_nm", [P, 2])
        ls = sb("d_ls", [P, 2])
        rl = sb("d_rl", [P, 2])
        o = sb("d_o", [DH, 2, TP])
        ident = sb("d_ident", [P, P])
        mask = sb("d_mask", [P, P])
        p_s = pb("d_p_s", [P, 2, 512])
        p_t = pb("d_p_t", [P, 2, 512])
        p_o = pb("d_p_o", [P, 2, 512])
        const_in = tl.sem("d_const_in")
        loaded = [tl.sem(f"d_loaded{k}") for k in range(2)]
        q_out = tl.sem("d_q_out")
        s_out = tl.sem("d_s_out")
        max_out = tl.sem("d_max_out")
        e_out = tl.sem("d_e_out")
        pr_out = tl.sem("d_pr_out")
        t_out = tl.sem("d_t_out")
        tc_out = tl.sem("d_tc_out")
        pv_out = tl.sem("d_pv_out")
        o_out = tl.sem("d_o_out")
        flight = tl.pool_sem("d_flight")
        stored = [tl.sem(f"d_stored{k}") for k in range(2)]

        def heads(eng, body):
            with eng.Fori(0, AH // 2) as r:
                for k in range(2):
                    body(2 * r + k, r, k)

        with nc.Block() as block:
            @block.sync
            def _(sp):
                sp.dma_start(ident[:, :], io["ident"]).then_inc(const_in, 16)
                sp.dma_start(mask[:, :], io["mask_qk"]).then_inc(const_in, 16)
                for k in range(2):
                    sp.dma_start(qa[DH + 1:DH + 2, k, :], io["ones_row"][:, 0:TP]).then_inc(const_in, 16)
                    sp.dma_start(ka[DH:DH + 1, k, :], io["ones_row"][:, 0:TP]).then_inc(const_in, 16)
                uh = dr["uT"].rearrange("a (h p) n -> (a h) p n", p=DH)

                def load(h, r, k):
                    sp.wait_ge(o_out, h + 1)
                    sp.dma_start(qraw[:, k, :], uh[ds(h + 2 * Q0, 1), :, 0:TP].rearrange("a p n -> (a p) n")).then_inc(loaded[k], 16)
                    sp.dma_start(ka[0:DH, k, :], uh[ds(h + 2 * K0, 1), :, 0:TP].rearrange("a p n -> (a p) n")).then_inc(loaded[k], 16)
                    sp.dma_start(qa[DH:DH + 1, k, :], dr["cum"][ds(h, 1), 0:TP]).then_inc(loaded[k], 16)
                    sp.dma_start(ka[DH + 1:KA, k, :], dr["ncum"][ds(h, 1), 0:TP]).then_inc(loaded[k], 16)
                    sp.dma_start(vv[:, k, :, :], dr["v_heads"][ds(h, 1), 0:TP, :].rearrange("a (c p) d -> p (a c) d", p=P)
                                 ).then_inc(loaded[k], 16)
                heads(sp, load)
            NLOAD = 80

            @block.vector
            def _(dve):
                v = nc.vector
                dve.wait_ge(const_in, 96)
                dve.sem_inc(o_out, 2)

                def head(h, r, k):
                    dve.wait_ge(loaded[k], NLOAD * r + NLOAD)
                    v.tensor_scalar(qa[0:DH, k, :], qraw[:, k, :], DH ** -0.5, None, ALU.mult).then_inc(q_out, 1)
                    for b in range(QB):
                        n = (b + 1) * P
                        s = b % 2
                        dve.wait_ge(s_out, 4 * h + b + 1)
                        v.tensor_tensor(p_s[:, s, n - P:n], p_s[:, s, n - P:n], mask[:, :], ALU.add)
                        dve.drain()
                        v.reduce_max(mx[:, s:s + 1], p_s[:, s, 0:n], AX)
                        dve.drain()
                        v.tensor_scalar(nm[:, s:s + 1], mx[:, s:s + 1], -1.0, None, ALU.mult).then_inc(max_out, 1)
                        dve.wait_ge(e_out, 4 * h + b + 1)
                        v.reciprocal(rl[:, s:s + 1], ls[:, s:s + 1])
                        dve.drain()
                        v.tensor_scalar(pr[:, s, 0:n], pr[:, s, 0:n], rl[:, s:s + 1], None, ALU.mult).then_inc(pr_out, 1)
                    dve.wait_ge(pv_out, 4 * h + 6)
                    dve.wait_ge(stored[k], 16 * r + 16)
                    v.tensor_copy(o[:, k, :], p_o[0:DH, k, :]).then_inc(o_out, 1)
                heads(dve, head)

            @block.scalar
            def _(act):
                def head(h, r, k):
                    for b in range(QB):
                        n = (b + 1) * P
                        s = b % 2
                        act.wait_ge(max_out, 4 * h + b + 1)
                        act.wait_ge(t_out, 4 * h + b + 1)
                        nc.scalar.activation(pr[:, s, 0:n], p_s[:, s, 0:n], ACT.Exp, bias=nm[:, s:s + 1], accum_out=ls[:, s:s + 1]
                                             ).then_inc(e_out, 1)
                        act.wait_ge(t_out, 4 * h + b + 3)
                        act.wait_ge(pv_out, 4 * h + b + 1)
                        nc.scalar.copy(pT[:, s, 0:b + 1, :], p_t[:, s, 0:n].rearrange("p (c q) -> p c q", q=P)).then_inc(tc_out, 1)
                heads(act, head)

            @block.tensor
            def _(pe):
                pe.wait_ge(const_in, 96)
                pe.sem_inc(t_out, 2)
                pe.sem_inc(pv_out, 2)

                def head(h, r, k):
                    pe.wait_ge(q_out, h + 1)
                    pe.wait_ge(o_out, h + 1)
                    for b in range(QB):
                        n = (b + 1) * P
                        s = b % 2
                        if b >= 2:
                            pe.wait_ge(e_out, 4 * h + b - 1)
                        nc.tensor.matmul(p_s[:, s, 0:n], qa[:, k, b * P:n], ka[:, k, 0:n], start=True, stop=True).then_inc(s_out, 1)
                        pe.wait_ge(pr_out, 4 * h + b + 1)
                        if b >= 2:
                            pe.wait_ge(tc_out, 4 * h + b - 1)
                        for c in range(b + 1):
                            last = nc.tensor.transpose(p_t[:, s, c * P:(c + 1) * P], pr[:, s, c * P:(c + 1) * P], ident[:, :])
                        last.then_inc(t_out, 1)
                        pe.wait_ge(tc_out, 4 * h + b + 1)
                        for c in range(b + 1):
                            last = nc.tensor.matmul(p_o[0:DH, k, b * P:n], vv[:, k, c, :], pT[:, s, c, :], start=(c == 0), stop=(c == b))
                        last.then_inc(pv_out, 1)
                heads(pe, head)

            @block.gpsimd
            def _(pool):
                for x in stored:
                    pool.sem_inc(x, 16)

                def store(h, r, k):
                    pool.wait_ge(o_out, h + 3)
                    tl.hold(pool, "d_pool")
                    pool.dma_start(dr["attT_heads"][ds(h, 1), :, 0:TP].rearrange("a p n -> (a p) n"), o[:, k, :]).then_inc(flight, 16)
                    pool.wait_ge(flight, 16 * h + 16)
                    pool.sem_inc(stored[k], 16)
                heads(pool, store)


def sample_attention(nc, tl, io, dr):
    RING = 4
    HQ = AH * TB
    with ExitStack() as ctx:
        sb = lambda n, s, d=F32: ctx.enter_context(nc.sbuf_tensor(n, s, d))
        pb = lambda n, s: ctx.enter_context(nc.psum_tensor(n, s, F32))
        q = sb("e_q", [P, 8, TB])
        kn = sb("e_kn", [P, 8, TB])
        vn = sb("e_vn", [TB, DA])
        ncn = sb("e_ncn", [AH, TB])
        pg = sb("e_pg", [P, NB * PAGES], I32)
        lane = sb("e_lane", [P, NB * PAGES], I32)
        ik_all = sb("e_ik_all", [P, NB * PAGES], I32)
        il_all = sb("e_il_all", [P, NB * PAGES], I32)
        ik = sb("e_ik", [P, 2, PAGES], I32)
        il = sb("e_il", [P, 2, PAGES], I32)
        lf = sb("e_lf", [AH, PAGES * PAGE])
        one = sb("e_one", [AH, PAGES * PAGE])
        rev = sb("e_rev", [AH, PAGES * PAGE])
        qp = sb("e_qp", [P, 8 * (P + 2 * TB)])
        kr = sb("e_kr", [P, RING, DA])
        vr = sb("e_vr", [P, RING, DA])
        pr = sb("e_pr", [P, PAGES * PAGE])
        prn = sb("e_prn", [P, TB])
        sn = sb("e_sn", [P, TB])
        st = sb("e_st", [P, 8])
        pT = sb("e_pT", [P, PAGES, P])
        pnT = sb("e_pnT", [TB, P])
        ov = sb("e_ov", [P, DA])
        oT = sb("e_oT", [P, 8, TB])
        ident = sb("e_ident", [P, P])
        sel = sb("e_sel", [AH, HQ])
        maskn = sb("e_maskn", [P, TB])
        p_s = pb("e_p_s", [P, 4, 512])
        p_n = pb("e_p_n", [P, 512])
        p_t = pb("e_p_t", [P, 512])
        p_o = pb("e_p_o", [P, 2, 512])
        const_in = tl.sem("e_const_in")
        loaded = tl.sem("e_loaded")
        lf_in = tl.pool_sem("e_lf_in")
        k_in = [tl.pool_sem(f"e_k_in{s}") for s in range(RING)]
        v_in = [tl.pool_sem(f"e_v_in{s}") for s in range(RING)]
        lane_out = tl.sem("e_lane_out")
        pg_in = tl.sem("e_pg_in")
        index_out = tl.sem("e_index_out")
        ik_out = tl.sem("e_ik_out")
        q_out = tl.sem("e_q_out")
        rev_out = tl.sem("e_rev_out")
        k_used = tl.sem("e_k_used")
        v_used = tl.sem("e_v_used")
        s_out = tl.sem("e_s_out")
        max_out = tl.sem("e_max_out")
        e_out = tl.sem("e_e_out")
        pr_out = tl.sem("e_pr_out")
        t_out = tl.sem("e_t_out")
        tc_out = tl.sem("e_tc_out")
        o_out = tl.sem("e_o_out")
        oc_out = tl.sem("e_oc_out")
        d_out = tl.sem("e_d_out")
        done = tl.sem("e_done")

        with nc.Block() as block:
            @block.sync
            def _(sp):
                sp.dma_start(ident[:, :], io["ident"]).then_inc(const_in, 16)
                sp.dma_start(sel[:, :], io["sel_hq"]).then_inc(const_in, 16)
                sp.dma_start(maskn[:, :], io["mask_new"]).then_inc(const_in, 16)
                sp.dma_start(pg[:, :], io["pages"].rearrange("b c -> (b c)").unsqueeze(0).to_broadcast([P, NB * PAGES])
                             ).then_inc(pg_in, 16)

                def load(b):
                    sp.dma_start(q[:, :, :], dr["uT"][Q0:Q0 + 8, :, ds(TB * b + TP, TB)].rearrange("a p n -> p a n")).then_inc(loaded, 16)
                    sp.dma_start(kn[:, :, :], dr["uT"][K0:K0 + 8, :, ds(TB * b + TP, TB)].rearrange("a p n -> p a n")).then_inc(loaded, 16)
                    sp.dma_start(vn[:, :], dr["v_tok"][ds(TB * b + TP, TB), :]).then_inc(loaded, 16)
                    sp.dma_start(ncn[:, :], dr["ncum"][:, ds(TB * b + TP, TB)]).then_inc(loaded, 16)

                def store(b):
                    sp.wait_ge(d_out, 2 * b + 4)
                    sp.dma_start(dr["attT"][:, :, ds(TB * b + TP, TB)].rearrange("a p n -> p a n"), oT[:, :, :]).then_inc(done, 16)
                load(0)
                with sp.Fori(1, NB) as b:
                    store(b - 1)
                    load(b)
                store(NB - 1)
                sp.wait_ge(done, 16 * NB + 16)
            NLOAD = 64

            @block.gpsimd
            def _(pool):
                g = nc.gpsimd
                g.iota(lane[:, :], pattern=[[0, NB * PAGES]], base=0, channel_multiplier=1).then_inc(lane_out, 1)
                pool.wait_ge(index_out, 1)

                def pages_k(b, par):
                    for c in range(PAGES):
                        pool.wait_ge(k_used, PAGES * b + c + 1)
                        tl.hold(pool, "e_pool")
                        pool.indirect_dma_start(kr[:, c % RING, :], None, io["cache_k"],
                                                bass.IndirectOffsetOnAxis(ik[:, par, c:c + 1], axis=0)).then_inc(k_in[c % RING], 16)

                def pages_v(b, par):
                    for c in range(PAGES):
                        pool.wait_ge(v_used, PAGES * b + c + 1)
                        tl.hold(pool, "e_pool")
                        pool.indirect_dma_start(vr[:, c % RING, :], None, io["cache_v"],
                                                bass.IndirectOffsetOnAxis(ik[:, par, c:c + 1], axis=0)).then_inc(v_in[c % RING], 16)

                def forgets(b, par):
                    g.tensor_copy(ik[:, par, :], ik_all[:, ds(PAGES * b, PAGES)]).then_inc(ik_out, 1)
                    g.tensor_copy(il[:, par, :], il_all[:, ds(PAGES * b, PAGES)]).then_inc(ik_out, 1)
                    pool.wait_ge(ik_out, 2 * b + 2)
                    pool.wait_ge(rev_out, b + 1)
                    tl.hold(pool, "e_pool")
                    for c in range(PAGES):
                        pool.indirect_dma_start(lf[:, c * PAGE:(c + 1) * PAGE], None, io["cache_f"],
                                                bass.IndirectOffsetOnAxis(il[0:AH, par, c:c + 1], axis=0)).then_inc(lf_in, 16)

                def sequence(b, par, more=True):
                    pages_k(b, par)
                    if more:
                        forgets(b + 1, 1 - par)
                    pages_v(b, par)
                forgets(0, 0)
                with pool.Fori(0, NB // 2 - 1) as b2:
                    sequence(2 * b2, 0)
                    sequence(2 * b2 + 1, 1)
                sequence(NB - 2, 0)
                sequence(NB - 1, 1, more=False)

            @block.vector
            def _(dve):
                v = nc.vector
                dve.sem_inc(d_out, 2)
                dve.sem_inc(done, 16)
                dve.sem_inc(rev_out, 1)
                v.memset(qp[:, :], 0.0)
                v.memset(one[:, :], 1.0)
                dve.wait_ge(const_in, 48)
                dve.wait_ge(lane_out, 1)
                dve.wait_ge(pg_in, 16)
                v.tensor_scalar(ik_all[:, :], pg[:, :], float(PAGE), None, ALU.mult)
                v.tensor_scalar(il_all[:, :], pg[:, :], float(AH), None, ALU.mult)
                dve.drain()
                v.tensor_tensor(ik_all[:, :], ik_all[:, :], lane[:, :], ALU.add)
                v.tensor_tensor(il_all[:, :], il_all[:, :], lane[:, :], ALU.add)
                dve.drain().then_inc(index_out, 1)
                with dve.Fori(0, NB) as b:
                    dve.wait_ge(loaded, NLOAD * b + NLOAD)
                    v.tensor_scalar(diagonal(qp, (0, DH), P, 8, 0, TB), q[0:DH, :, :], DH ** -0.5, None, ALU.mult)
                    v.tensor_scalar(diagonal(qp, (DH, P), P, 8, TB, TB), q[DH:P, :, :], DH ** -0.5, None, ALU.mult)
                    dve.drain().then_inc(q_out, 1)
                    dve.wait_ge(lf_in, 16 * PAGES * b + 16 * PAGES)
                    v.tensor_tensor_scan(rev[:, :], one[:, :], lf[:, :], 0.0, ALU.mult, ALU.add)
                    dve.drain()
                    v.tensor_tensor(rev[:, :], rev[:, :], lf[:, :], ALU.subtract).then_inc(rev_out, 1)
                    dve.wait_ge(s_out, b + 1)
                    v.tensor_tensor(sn[:, :], p_n[:, 0:TB], maskn[:, :], ALU.add)
                    v.reduce_max(st[:, 0:1], p_s[:, :, :].rearrange("p a n -> p (a n)"), AX)
                    dve.drain()
                    v.reduce_max(st[:, 1:2], sn[:, :], AX)
                    dve.drain()
                    v.tensor_tensor(st[:, 2:3], st[:, 0:1], st[:, 1:2], ALU.max)
                    dve.drain()
                    v.tensor_scalar(st[:, 3:4], st[:, 2:3], -1.0, None, ALU.mult).then_inc(max_out, 1)
                    dve.wait_ge(e_out, b + 1)
                    v.tensor_tensor(st[:, 6:7], st[:, 4:5], st[:, 5:6], ALU.add)
                    dve.drain()
                    v.reciprocal(st[:, 7:8], st[:, 6:7])
                    dve.drain()
                    v.tensor_scalar(pr[:, :], pr[:, :], st[:, 7:8], None, ALU.mult)
                    v.tensor_scalar(prn[:, :], prn[:, :], st[:, 7:8], None, ALU.mult)
                    dve.drain().then_inc(pr_out, 1)
                    for u in range(2):
                        dve.wait_ge(t_out, 7 * b + 6 + u)
                        if u == 0:
                            dve.wait_ge(done, 16 * b + 16)
                        tv = p_t[:, :].rearrange("p (j c) -> p j c", c=P)
                        for lo, off in ((0, 0), (DH, TB)):
                            for j in range(4):
                                jj = 4 * u + j
                                v.tensor_copy(oT[lo:lo + DH, jj, :], tv[lo:lo + DH, j, 2 * TB * jj + off:2 * TB * jj + off + TB])
                        dve.drain().then_inc(d_out, 1)

            @block.scalar
            def _(act):
                with act.Fori(0, NB) as b:
                    act.wait_ge(max_out, b + 1)
                    nc.scalar.activation(pr[:, :], p_s[:, :, :].rearrange("p a n -> p (a n)"), ACT.Exp, bias=st[:, 3:4],
                                         accum_out=st[:, 4:5])
                    nc.scalar.activation(prn[:, :], sn[:, :], ACT.Exp, bias=st[:, 3:4], accum_out=st[:, 5:6]).then_inc(e_out, 1)
                    for u in range(4):
                        act.wait_ge(t_out, 7 * b + u + 1)
                        nc.scalar.copy(pT[:, 4 * u:4 * u + 4, :], p_t[:, :].rearrange("p (c q) -> p c q", q=P)).then_inc(tc_out, 1)
                    act.wait_ge(t_out, 7 * b + 5)
                    nc.scalar.copy(pnT[:, :], p_n[0:TB, P:2 * P]).then_inc(tc_out, 1)
                    act.wait_ge(o_out, b + 1)
                    nc.scalar.copy(ov[:, :], p_o[:, :, :].rearrange("p a n -> p (a n)")).then_inc(oc_out, 1)

            @block.tensor
            def _(pe):
                pe.wait_ge(const_in, 48)
                pe.sem_inc(k_used, RING)
                pe.sem_inc(v_used, RING)
                with pe.Fori(0, NB) as b:
                    pe.wait_ge(q_out, b + 1)
                    pe.wait_ge(rev_out, b + 2)
                    pe.wait_ge(loaded, NLOAD * b + NLOAD)
                    tl.hold(pe, "e_pe")
                    for c in range(PAGES):
                        bank = p_s[:, c // 4, :]
                        pe.wait_ge(k_in[c % RING], 16 * (PAGES // RING) * b + 16 * (c // RING) + 16)
                        for j in range(8):
                            last = nc.tensor.matmul(bank[:, (c % 4) * PAGE:(c % 4 + 1) * PAGE], qp[:, j * P:(j + 1) * P],
                                                    kr[:, c % RING, j * P:(j + 1) * P], start=(j == 0 and c % 4 == 0), stop=False,
                                                    skip_group_check=True)
                        last.then_inc(k_used, 1)
                        if c % 4 == 3:
                            nc.tensor.matmul(bank, sel[:, :], rev[:, (c - 3) * PAGE:(c + 1) * PAGE], start=False, stop=True,
                                             skip_group_check=True)
                    for j in range(8):
                        nc.tensor.matmul(p_n[:, 0:TB], qp[:, j * P:(j + 1) * P], kn[:, j, :], start=(j == 0), stop=False)
                    nc.tensor.matmul(p_n[:, 0:TB], sel[:, :], ncn[:, :], start=False, stop=True).then_inc(s_out, 1)
                    pe.wait_ge(pr_out, b + 1)
                    pe.wait_ge(d_out, 2 * b + 2)
                    for u in range(4):
                        if u:
                            pe.wait_ge(tc_out, 5 * b + u)
                        for c in range(4 * u, 4 * u + 4):
                            last = nc.tensor.transpose(p_t[:, (c % 4) * P:(c % 4 + 1) * P], pr[:, c * PAGE:(c + 1) * PAGE], ident[:, :])
                        last.then_inc(t_out, 1)
                    nc.tensor.transpose(p_n[0:TB, P:2 * P], prn[:, :], ident[:, :]).then_inc(t_out, 1)
                    pe.wait_ge(tc_out, 5 * b + 5)
                    for c in range(PAGES):
                        pe.wait_ge(v_in[c % RING], 16 * (PAGES // RING) * b + 16 * (c // RING) + 16)
                        for h in range(2):
                            last = nc.tensor.matmul(p_o[:, h, :], pT[:, c, :], vr[:, c % RING, h * 512:(h + 1) * 512],
                                                    start=(c == 0), stop=False)
                        last.then_inc(v_used, 1)
                    for h in range(2):
                        last = nc.tensor.matmul(p_o[:, h, :], pnT[:, :], vn[:, h * 512:(h + 1) * 512], start=False, stop=True)
                    last.then_inc(o_out, 1)
                    pe.wait_ge(oc_out, b + 1)
                    for u in range(2):
                        if u:
                            pe.wait_ge(d_out, 2 * b + 3)
                        for j in range(4 * u, 4 * u + 4):
                            last = nc.tensor.transpose(p_t[:, (j % 4) * P:(j % 4 + 1) * P], ov[:, j * P:(j + 1) * P], ident[:, :])
                        last.then_inc(t_out, 1)


def merge(nc, tl, io, dr):
    NTL = D // P
    KA = DA // P
    with ExitStack() as ctx:
        sb = lambda n, s: ctx.enter_context(nc.sbuf_tensor(n, s, F32))
        aT = sb("f_aT", [P, KA, T])
        mT = sb("f_mT", [P, KT, T])
        wa = sb("f_wa", [P, 2, KA, P])
        ws = sb("f_ws", [P, 2, KT, P])
        ga = sb("f_ga", [P, 2, T])
        gs = sb("f_gs", [P, 2, T])
        mix = sb("f_mix", [P, 2, T])
        t2 = sb("f_t2", [P, 2, T])
        acc = ctx.enter_context(nc.psum_tensor("f_acc", [P, 2, 4, 512], F32))
        x_in = tl.sem("f_x_in")
        w_in = [tl.sem(f"f_w_in{k}") for k in range(2)]
        gate_out = tl.sem("f_gate_out")
        product = tl.sem("f_product")
        mixed = tl.sem("f_mixed")
        flight = tl.pool_sem("f_flight")
        stored = [tl.sem(f"f_stored{k}") for k in range(2)]

        def tiles(eng, body):
            with eng.Fori(0, NTL // 2) as r:
                for k in range(2):
                    body(2 * r + k, r, k)

        with nc.Block() as block:
            @block.sync
            def _(sp):
                sp.dma_start(aT[:, :, :], dr["attT"].rearrange("a p n -> p a n")).then_inc(x_in, 16)
                sp.dma_start(mT[:, :, :], dr["mT"].rearrange("a p n -> p a n")).then_inc(x_in, 16)

                def load(n, r, k):
                    sp.wait_ge(mixed, n + 1)
                    sp.dma_start(wa[:, k, :, :], io["w_ba"][ds(n, 1)].rearrange("a p k n -> (a p) k n")).then_inc(w_in[k], 16)
                    sp.dma_start(ws[:, k, :, :], io["w_bs"][ds(n, 1)].rearrange("a p k n -> (a p) k n")).then_inc(w_in[k], 16)
                    sp.dma_start(ga[:, k, :], dr["uT"][ds(n + GA0, 1)].rearrange("a p n -> (a p) n")).then_inc(w_in[k], 16)
                    sp.dma_start(gs[:, k, :], dr["uT"][ds(n + GS0, 1)].rearrange("a p n -> (a p) n")).then_inc(w_in[k], 16)
                tiles(sp, load)

            @block.tensor
            def _(pe):
                pe.wait_ge(x_in, 32)

                def products(n, r, k):
                    pe.wait_ge(w_in[k], 64 * r + 64)
                    pe.wait_ge(mixed, n + 1)
                    for kk in range(KA):
                        for h in range(2):
                            nc.tensor.matmul(acc[:, k, h, 0:HALF], wa[:, k, kk, :], aT[:, kk, h * HALF:(h + 1) * HALF],
                                             start=(kk == 0), stop=(kk == KA - 1))
                    for kk in range(KT):
                        for h in range(2):
                            last = nc.tensor.matmul(acc[:, k, 2 + h, 0:HALF], ws[:, k, kk, :], mT[:, kk, h * HALF:(h + 1) * HALF],
                                                    start=(kk == 0), stop=(kk == KT - 1))
                    last.then_inc(product, 1)
                tiles(pe, products)

            @block.scalar
            def _(act):
                def gates(n, r, k):
                    act.wait_ge(w_in[k], 64 * r + 64)
                    nc.scalar.activation(ga[:, k, :], ga[:, k, :], ACT.Sigmoid)
                    nc.scalar.activation(gs[:, k, :], gs[:, k, :], ACT.Sigmoid)
                    act.drain().then_inc(gate_out, 1)
                tiles(act, gates)

            @block.vector
            def _(dve):
                v = nc.vector
                dve.sem_inc(mixed, 2)

                def mixing(n, r, k):
                    dve.wait_ge(gate_out, n + 1)
                    dve.wait_ge(product, n + 1)
                    dve.wait_ge(stored[k], 16 * r + 16)
                    halves = lambda x: x.rearrange("p (h c) -> p h c", h=2)
                    v.tensor_tensor(halves(mix[:, k, :]), acc[:, k, 0:2, 0:HALF], halves(ga[:, k, :]), ALU.mult)
                    v.tensor_tensor(halves(t2[:, k, :]), acc[:, k, 2:4, 0:HALF], halves(gs[:, k, :]), ALU.mult)
                    dve.drain()
                    v.tensor_tensor(mix[:, k, :], mix[:, k, :], t2[:, k, :], ALU.add).then_inc(mixed, 1)
                tiles(dve, mixing)

            @block.gpsimd
            def _(pool):
                for x in stored:
                    pool.sem_inc(x, 16)

                def store(n, r, k):
                    pool.wait_ge(mixed, n + 3)
                    tl.hold(pool, "f_pool")
                    pool.dma_start(dr["mixT"][ds(n, 1)].rearrange("a p n -> (a p) n"), mix[:, k, :]).then_inc(flight, 16)
                    pool.wait_ge(flight, 16 * n + 16)
                    pool.sem_inc(stored[k], 16)
                tiles(pool, store)


def out_norm(nc, tl, io, dr):
    with ExitStack() as ctx:
        sb = lambda n, s: ctx.enter_context(nc.sbuf_tensor(n, s, F32))
        wo = sb("g_wo", [P, KT, D])
        mt = sb("g_mt", [P, KT, P])
        xt = sb("g_xt", [P, D])
        rr = sb("g_rr", [P, D])
        gb = sb("g_gb", [P, 2, D])
        xs = sb("g_xs", [P, KT, P])
        st = sb("g_st", [P, 8])
        ident = sb("g_ident", [P, P])
        acc = ctx.enter_context(nc.psum_tensor("g_acc", [P, 4, 512], F32))
        p_t = ctx.enter_context(nc.psum_tensor("g_p_t", [P, 4, 512], F32))
        const_in = tl.sem("g_const_in")
        m_in = tl.sem("g_m_in")
        t_in = tl.sem("g_t_in")
        product = tl.sem("g_product")
        summed = tl.sem("g_summed")
        squares = tl.sem("g_squares")
        var_out = tl.sem("g_var_out")
        root_out = tl.sem("g_root_out")
        normed = tl.sem("g_normed")
        turned = tl.sem("g_turned")
        copied = tl.sem("g_copied")
        flight = tl.pool_sem("g_flight")
        stored = tl.sem("g_stored")

        def tiles(eng, body):
            with eng.Fori(0, 4) as i:
                body(i, P)
            body(4, TS)

        with nc.Block() as block:
            @block.sync
            def _(sp):
                sp.dma_start(ident[:, :], io["ident"]).then_inc(const_in, 16)
                for i, name in enumerate(("ln1_g", "ln1_b")):
                    sp.dma_start(gb[:, i, :], io[name].to_broadcast([P, D])).then_inc(const_in, 16)
                for k in range(4):
                    sp.dma_start(wo[:, 4 * k:4 * k + 4, :], io["w_out"][:, 4 * k:4 * k + 4, :]).then_inc(const_in, 16)

                def load(i, n):
                    sp.wait_ge(product, i + 1)
                    sp.dma_start(mt[:, :, 0:n], dr["mixT"][:, :, ds(i * P, n)].rearrange("k p n -> p k n")).then_inc(m_in, 16)
                    sp.wait_ge(summed, i + 1)
                    sp.dma_start(xt[0:n, :], io["x_tok"][ds(i * P, n), :]).then_inc(t_in, 16)
                tiles(sp, load)

            @block.tensor
            def _(pe):
                pe.sem_inc(product, 1)
                pe.sem_inc(turned, 1)
                pe.wait_ge(const_in, 112)

                def products(i, n):
                    pe.wait_ge(m_in, i * 16 + 16)
                    pe.wait_ge(summed, i + 1)
                    if n < P:
                        tl.hold(pe, "g_pe")
                    for c in range(4):
                        for k in range(KT):
                            last = nc.tensor.matmul(acc[0:n, c, :], mt[:, k, 0:n], wo[:, k, c * 512:(c + 1) * 512],
                                                    start=(k == 0), stop=(k == KT - 1))
                    last.then_inc(product, 1)
                    pe.wait_ge(normed, i + 1)
                    tl.hold(pe, "g_pe")
                    for k in range(KT):
                        last = nc.tensor.transpose(p_t[:, k // 4, (k % 4) * P:(k % 4) * P + n], xt_out(k, n), ident[0:n, 0:n])
                    last.then_inc(turned, 1)
                xt_out = lambda k, n: rr[0:n, k * P:(k + 1) * P]
                tiles(pe, products)

            @block.vector
            def _(dve):
                v = nc.vector
                dve.sem_inc(summed, 1)
                dve.wait_ge(const_in, 112)

                def norm(i, n):
                    dve.wait_ge(product, i + 2)
                    dve.wait_ge(t_in, i * 16 + 16)
                    dve.wait_ge(turned, i + 1)
                    dve.wait_ge(stored, i * 32 + 32)
                    v.scalar_tensor_tensor(rr[0:n, :], xt[0:n, :], ALPHA, acc[0:n, :, :].rearrange("p a n -> p (a n)"),
                                           ALU.mult, ALU.add, accum_out=st[0:n, 0:1])
                    dve.drain().then_inc(summed, 1)
                    layer_norm_steps(nc, dve, rr, gb, st, n, i, squares, var_out, root_out)
                    dve.drain().then_inc(normed, 1)
                tiles(dve, norm)

            @block.scalar
            def _(act):
                def roots(i, n):
                    act.wait_ge(var_out, 2 * i + 1)
                    act.wait_ge(stored, i * 32 + 32)
                    nc.scalar.activation(xs_flat(n), rr[0:n, :], ACT.Square, bias=st[0:n, 1:2], accum_out=st[0:n, 2:3]
                                         ).then_inc(squares, 1)
                    act.wait_ge(var_out, 2 * i + 2)
                    nc.scalar.activation(st[0:n, 4:5], st[0:n, 3:4], ACT.Sqrt).then_inc(root_out, 1)
                    act.wait_ge(turned, i + 2)
                    nc.scalar.copy(xs[:, :, 0:n], p_t[:, :, :].rearrange("p a (b c) -> p (a b) c", c=P)[:, :, 0:n]).then_inc(copied, 1)
                xs_flat = lambda n: xs[0:n, :, :].rearrange("p k c -> p (k c)")
                tiles(act, roots)

            @block.gpsimd
            def _(pool):
                pool.sem_inc(stored, 32)

                def store(i, n):
                    pool.wait_ge(normed, i + 1)
                    tl.hold(pool, "g_pool")
                    pool.dma_start(dr["x1"][ds(i * P, n), :], rr[0:n, :]).then_inc(flight, 16)
                    pool.wait_ge(copied, i + 1)
                    tl.hold(pool, "g_pool")
                    pool.dma_start(dr["x1T"][:, :, ds(i * P, n)].rearrange("k p n -> p k n"), xs[:, :, 0:n]).then_inc(flight, 16)
                    pool.wait_ge(flight, 32 * i + 32)
                    pool.sem_inc(stored, 32)
                tiles(pool, store)


def layer_norm_steps(nc, dve, rr, gb, st, n, i, squares, var_out, root_out):
    v = nc.vector
    v.tensor_scalar(st[0:n, 1:2], st[0:n, 0:1], -1.0 / D, None, ALU.mult).then_inc(var_out, 1)
    dve.wait_ge(squares, i + 1)
    v.tensor_scalar(st[0:n, 3:4], st[0:n, 2:3], 1.0 / D, EPS, ALU.mult, ALU.add).then_inc(var_out, 1)
    dve.wait_ge(root_out, i + 1)
    v.reciprocal(st[0:n, 5:6], st[0:n, 4:5])
    dve.drain()
    v.tensor_scalar(rr[0:n, :], rr[0:n, :], st[0:n, 1:2], st[0:n, 5:6], ALU.add, ALU.mult)
    dve.drain()
    v.tensor_tensor(rr[0:n, :], rr[0:n, :], gb[0:n, 0, :], ALU.mult)
    dve.drain()
    v.tensor_tensor(rr[0:n, :], rr[0:n, :], gb[0:n, 1, :], ALU.add)


def queries(nc, tl, io, dr):
    NTL = D // P
    with ExitStack() as ctx:
        sb = lambda n, s, d=F32: ctx.enter_context(nc.sbuf_tensor(n, s, d))
        xT = sb("h_xT", [P, KT, T])
        xh = sb("h_xh", [P, KT, T], F32R)
        xl = sb("h_xl", [P, KT, T], F32R)
        w = sb("h_w", [P, 4, KT * P])
        wh = sb("h_wh", [P, 2, KT * P], F32R)
        wl = sb("h_wl", [P, 2, KT * P], F32R)
        out = sb("h_out", [P, 4, T])
        acc = ctx.enter_context(nc.psum_tensor("h_acc", [P, 8, 512], F32))
        x_in = tl.sem("h_x_in")
        w_in = [tl.sem(f"h_w_in{k}") for k in range(4)]
        xh_out = tl.sem("h_xh_out")
        xl_out = tl.sem("h_xl_out")
        wh_out = tl.sem("h_wh_out")
        w_split = tl.sem("h_w_split")
        tile_done = tl.sem("h_tile_done")
        copied_a = tl.sem("h_copied_a")
        copied_v = tl.sem("h_copied_v")
        flight = tl.pool_sem("h_flight")
        stored = [tl.sem(f"h_stored{k}") for k in range(4)]

        def tiles(eng, body):
            with eng.Fori(0, NTL // 4) as r:
                for k in range(4):
                    body(4 * r + k, r, k)

        def converter(eng, split, copy):
            split(0, 0, 0)
            with eng.Fori(0, NTL // 4 - 1) as r:
                for k in range(4):
                    split(4 * r + k + 1, r if k < 3 else r + 1, (k + 1) % 4)
                    copy(4 * r + k, r, k)
            for k in range(4):
                if k < 3:
                    split(NTL - 4 + k + 1, NTL // 4 - 1, k + 1)
                copy(NTL - 4 + k, NTL // 4 - 1, k)

        with nc.Block() as block:
            @block.sync
            def _(sp):
                sp.dma_start(xT[:, :, :], dr["x1T"].rearrange("k p n -> p k n")).then_inc(x_in, 16)

                def load(n, r, k):
                    sp.wait_ge(w_split, n + 1)
                    sp.dma_start(w[:, k, :], io["w_query"][ds(n, 1)].rearrange("a p k n -> (a p) (k n)")).then_inc(w_in[k], 16)
                tiles(sp, load)

            @block.tensor
            def _(pe):
                pe.sem_inc(tile_done, 4)
                pe.wait_ge(xl_out, 1)

                def products(n, r, k):
                    pe.wait_ge(w_split, n + 5)
                    pe.wait_ge(copied_a, n + 1)
                    pe.wait_ge(copied_v, n + 1)
                    for kk in range(KT):
                        for weights, x in ((wh, xh), (wh, xl), (wl, xh)):
                            for h in range(2):
                                last = nc.tensor.matmul(acc[:, 2 * k + h, 0:HALF], weights[:, k % 2, kk * P:(kk + 1) * P],
                                                        x[:, kk, h * HALF:(h + 1) * HALF],
                                                        start=(kk == 0 and x is xh and weights is wh),
                                                        stop=(kk == KT - 1 and weights is wl))
                    last.then_inc(tile_done, 1)
                tiles(pe, products)

            @block.scalar
            def _(act):
                act.sem_inc(copied_a, 4)
                act.wait_ge(x_in, 16)
                nc.scalar.copy(xh[:, :, :], xT[:, :, :]).then_inc(xh_out, 1)

                def split(n, r, k):
                    act.wait_ge(w_in[k], 16 * r + 16)
                    act.wait_ge(tile_done, n + 3)
                    nc.scalar.copy(wh[:, k % 2, :], w[:, k, :]).then_inc(wh_out, 1)

                def copy(n, r, k):
                    act.wait_ge(tile_done, n + 5)
                    act.wait_ge(stored[k], 16 * r + 16)
                    nc.scalar.copy(out[:, k, 0:HALF], acc[:, 2 * k, 0:HALF]).then_inc(copied_a, 1)
                converter(act, split, copy)

            @block.vector
            def _(dve):
                dve.sem_inc(copied_v, 4)
                dve.sem_inc(w_split, 4)
                dve.wait_ge(xh_out, 1)
                nc.vector.tensor_tensor(xl[:, :, :], xT[:, :, :], xh[:, :, :], ALU.subtract).then_inc(xl_out, 1)

                def split(n, r, k):
                    dve.wait_ge(wh_out, n + 1)
                    nc.vector.tensor_tensor(wl[:, k % 2, :], w[:, k, :], wh[:, k % 2, :], ALU.subtract).then_inc(w_split, 1)

                def copy(n, r, k):
                    dve.wait_ge(tile_done, n + 5)
                    dve.wait_ge(stored[k], 16 * r + 16)
                    nc.vector.tensor_copy(out[:, k, HALF:T], acc[:, 2 * k + 1, 0:HALF]).then_inc(copied_v, 1)
                converter(dve, split, copy)

            @block.gpsimd
            def _(pool):
                for x in stored:
                    pool.sem_inc(x, 16)

                def store(n, r, k):
                    pool.wait_ge(copied_a, n + 5)
                    pool.wait_ge(copied_v, n + 5)
                    tl.hold(pool, "h_pool")
                    pool.dma_start(dr["qT"][ds(n, 1)].rearrange("a p n -> (a p) n"), out[:, k, :]).then_inc(flight, 16)
                    pool.wait_ge(flight, 16 * n + 16)
                    pool.sem_inc(stored[k], 16)
                tiles(pool, store)


def peer(nc, tl, io, dr):
    S = 2 * PH
    UNR, VR = 8, 4
    TURNS = PICKS // UNR
    LEAD = 2
    HP = PICKS // 2
    NTILE = len(TT)
    with ExitStack() as ctx:
        sb = lambda n, s, d=F32: ctx.enter_context(nc.sbuf_tensor(n, s, d))
        qt = sb("i_qt", [P, S, P])
        sk = sb("i_sk", [P, S, NK])
        s1 = sb("i_s1", [P, S, NK])
        eq = sb("i_eq", [P, PH, TOPK, TOPK])
        tv = sb("i_tv", [P, S, TOPK])
        ti = sb("i_ti", [P, S, TOPK], U32)
        tf = sb("i_tf", [P, S, TOPK])
        bv = sb("i_bv", [P, PH, TOPK])
        bi = sb("i_bi", [P, PH, TOPK], U32)
        ba = sb("i_ba", [P, PH, TOPK], U32)
        bf = sb("i_bf", [P, 2, PH, TOPK])
        ex = sb("i_ex", [P, 2, PICKS])
        ei = sb("i_ei", [P, PICKS], I32)
        ew = sb("i_ew", [P, PICKS], I32)
        eu = sb("i_eu", [P, 2, UNR], I32)
        ev = sb("i_ev", [P, 2, UNR], I32)
        gt = sb("i_gt", [P, PICKS])
        sm = sb("i_sm", [P, 2, PH])
        au = sb("i_au", [P, PICKS])
        as_ = sb("i_as", [P, UNR])
        cf = sb("i_cf", [P, PICKS])
        cs = sb("i_cs", [P, UNR])
        dg = sb("i_dg", [P, VR, P])
        iota = sb("i_iota", [P, TOPK])
        ident = sb("i_ident", [P, P])
        fold = sb("i_fold", [P, P])
        x1 = sb("i_x1", [P, D])
        urow = sb("i_urow", [P, UNR, D])
        vrow = sb("i_vrow", [P, VR, D])
        ax = sb("i_ax", [P, D])
        rr = sb("i_rr", [P, D])
        junk = sb("i_junk", [P, D])
        gb = sb("i_gb", [P, 2, D])
        st = sb("i_st", [P, 8])
        p_s = ctx.enter_context(nc.psum_tensor("i_p_s", [P, 4, 512], F32))
        p_f = ctx.enter_context(nc.psum_tensor("i_p_f", [P, 4, 512], F32))
        const_in = tl.sem("i_const_in")
        q_in = tl.sem("i_q_in")
        scored = tl.sem("i_scored")
        s_copied = tl.sem("i_s_copied")
        best = tl.sem("i_best")
        gate_e = tl.sem("i_gate_e")
        index_out = tl.sem("i_index_out")
        ucol = tl.sem("i_ucol")
        vcol = tl.sem("i_vcol")
        u_in = [tl.pool_sem(f"i_u_in{k}") for k in range(UNR)]
        v_in = [tl.pool_sem(f"i_v_in{k}") for k in range(VR)]
        u_used = tl.sem("i_u_used")
        v_used = tl.sem("i_v_used")
        act_in = tl.sem("i_act_in")
        gelu_out = tl.sem("i_gelu_out")
        handed = tl.sem("i_handed")
        diag_out = tl.sem("i_diag_out")
        squares = tl.sem("i_squares")
        var_out = tl.sem("i_var_out")
        root_out = tl.sem("i_root_out")
        normed = tl.sem("i_normed")
        flight = tl.pool_sem("i_flight")
        stored = tl.sem("i_stored")

        moved_i = tl.sem("i_moved_i")
        moved_g = tl.sem("i_moved_g")
        gates_out = tl.sem("i_gates_out")

        def steps(eng, body):
            body(0, P, 0, TURNS, 0)
            with eng.Fori(1, NTILE - 1) as j:
                body(j, P, P, TURNS, TURNS)
            body(NTILE - 1, TS, P, TURNS // 2, TURNS)
            body(NTILE, 0, TS, 0, TURNS // 2)

        with nc.Block() as block:
            @block.sync
            def _(sp):
                sp.dma_start(ident[:, :], io["ident"]).then_inc(const_in, 16)
                sp.dma_start(iota[:, :], io["iota16"]).then_inc(const_in, 16)
                sp.dma_start(fold[:, :], io["fold"]).then_inc(const_in, 16)
                sp.dma_start(sk[:, :, :], io["keysT"]).then_inc(const_in, 16)
                for i, name in enumerate(("ln2_g", "ln2_b")):
                    sp.dma_start(gb[:, i, :], io[name].to_broadcast([P, D])).then_inc(const_in, 16)

                def load(j, n, _, tu, tv_):
                    if n:
                        sp.wait_ge(scored, j + 1)
                        sp.dma_start(qt[:, :, 0:n], dr["qT"][:, :, ds(j * P, n)].rearrange("k p n -> p k n")).then_inc(q_in, 16)
                        sp.wait_ge(handed, j + 1)
                        sp.dma_start(x1[0:n, :], dr["x1"][ds(j * P, n), :]).then_inc(q_in, 16)
                        if n < P:
                            sp.dma_start(x1[n:P, :], dr["x1"][ds(j * P, n), :]).then_inc(q_in, 16)
                            sp.wait_ge(index_out, j + 1)
                            sp.dma_start(ei[n:P, 0:HP], ei[0:n, HP:PICKS]).then_inc(moved_i, 16)
                            sp.wait_ge(gates_out, j + 1)
                            sp.dma_start(gt[n:P, 0:HP], gt[0:n, HP:PICKS]).then_inc(moved_g, 16)
                steps(sp, load)

            @block.tensor
            def _(pe):
                pe.sem_inc(scored, 1)
                pe.sem_inc(v_used, VR)
                pe.wait_ge(const_in, 96)

                def step(j, nu, n, tu, tv_):
                    if nu:
                        pe.wait_ge(q_in, 32 * j + (32 if nu == P else 48))
                        tl.hold(pe, "i_pe")
                        for i in range(S):
                            last = nc.tensor.matmul(p_s[0:nu, i // 4, (i % 4) * NK:(i % 4 + 1) * NK], qt[:, i, 0:nu], sk[:, i, :],
                                                    start=True, stop=True)
                        last.then_inc(scored, 1)
                    if n:
                        def turn(c, first, stop):
                            for u in range(UNR):
                                pe.wait_ge(diag_out, (j - 1) * PICKS + c * UNR + u + 1)
                                pe.wait_ge(v_in[u % VR], 16 * ((j - 1) * (PICKS // VR) + c * (UNR // VR) + u // VR) + 16)
                                tl.hold(pe, "i_pe")
                                for b in range(4):
                                    last = nc.tensor.matmul(p_f[:, b, :], dg[:, u % VR, :], vrow[:, u % VR, b * 512:(b + 1) * 512],
                                                            start=(first and u == 0), stop=(stop and u == UNR - 1), skip_group_check=True)
                                last.then_inc(v_used, 1)
                        turn(0, True, False)
                        with pe.Fori(1, tv_ - 1) as c:
                            turn(c, False, False)
                        turn(tv_ - 1, False, True)
                steps(pe, step)

            @block.gpsimd
            def _(pool):
                def step(j, nu, nv, tu, tv_):
                    def turn(c, k, u_too, v_turn):
                        if u_too:
                            nc.gpsimd.tensor_copy(eu[:, k, :], ei[:, ds(c * UNR, UNR)]).then_inc(ucol, 1)
                        if v_turn is not None:
                            nc.gpsimd.tensor_copy(ev[:, k, :], ew[:, ds(v_turn * UNR, UNR)]).then_inc(vcol, 1)
                        for u in range(UNR):
                            if u_too:
                                if u == 0:
                                    pool.wait_ge(ucol, TURNS * j + c + 1)
                                pool.wait_ge(u_used, PICKS * j + c * UNR + u + 1)
                                tl.hold(pool, "i_pool")
                                pool.indirect_dma_start(urow[:, u, :], None, io["expert_u"],
                                                        bass.IndirectOffsetOnAxis(eu[:, k, u:u + 1], axis=0)).then_inc(u_in[u], 16)
                            if v_turn is not None:
                                if u == 0:
                                    pool.wait_ge(vcol, TURNS * (j - 1) + v_turn + 1)
                                pool.wait_ge(v_used, PICKS * (j - 1) + v_turn * UNR + u + 1)
                                tl.hold(pool, "i_pool")
                                pool.indirect_dma_start(vrow[:, u % VR, :], None, io["expert_v"],
                                                        bass.IndirectOffsetOnAxis(ev[:, k, u:u + 1], axis=0)).then_inc(v_in[u % VR], 16)

                    if nv:
                        pool.wait_ge(handed, j + 1)
                        tl.hold(pool, "i_pool")
                        with pool.Fori(0, (LEAD if nu else tv_) // 2) as c2:
                            for k in range(2):
                                turn(None, k, False, 2 * c2 + k)
                    if nu:
                        pool.wait_ge(index_out, j + 1)
                        tl.hold(pool, "i_pool")
                        if nu < P:
                            pool.wait_ge(moved_i, 16)
                            tl.hold(pool, "i_pool")
                        joint = min(tu, tv_ - LEAD) if nv else 0
                        if joint:
                            with pool.Fori(0, joint // 2) as c2:
                                for k in range(2):
                                    turn(2 * c2 + k, k, True, 2 * c2 + k + LEAD)
                        if joint < tu:
                            with pool.Fori(joint // 2, tu // 2) as c2:
                                for k in range(2):
                                    turn(2 * c2 + k, k, True, None)
                        if nv and LEAD + joint < tv_:
                            with pool.Fori((LEAD + joint) // 2, tv_ // 2) as c2:
                                for k in range(2):
                                    turn(None, k, False, 2 * c2 + k)
                        pool.wait_ge(u_used, PICKS * j + tu * UNR + UNR)
                        tl.hold(pool, "i_pool")
                    if nv:
                        pool.wait_ge(v_used, PICKS * (j - 1) + tv_ * UNR + VR)
                        tl.hold(pool, "i_pool")
                        pool.wait_ge(normed, j)
                        tl.hold(pool, "i_pool")
                        pool.dma_start(dr["y"][ds((j - 1) * P, nv), :], rr[0:nv, :]).then_inc(flight, 16)
                        pool.wait_ge(flight, 16 * (j - 1) + 16)
                        pool.sem_inc(stored, 16)
                pool.sem_inc(stored, 16)
                steps(pool, step)

            @block.scalar
            def _(act):
                def step(j, nu, nv, tu, tv_):
                    def diagonals(lo, hi):
                        with act.Fori(lo, hi) as c:
                            act.drain()
                            nc.scalar.copy(cs[:, :], cf[:, ds(c * UNR, UNR)])
                            act.drain()
                            for u in range(UNR):
                                act.wait_ge(v_used, PICKS * (j - 1) + c * UNR + u + 1)
                                nc.scalar.activation(dg[:, u % VR, :], (ident if nv == P else fold)[:, :], ACT.Copy, scale=cs[:, u:u + 1]
                                                     ).then_inc(diag_out, 1)
                    if nu:
                        act.wait_ge(scored, j + 2)
                        nc.scalar.copy(s1[0:nu, :, :], p_s[0:nu, :, :].rearrange("p a (b c) -> p (a b) c", c=NK)).then_inc(s_copied, 1)
                    if nv:
                        act.wait_ge(handed, j + 1)
                        diagonals(0, LEAD)
                    if nu:
                        act.wait_ge(best, j + 1)
                        nc.scalar.activation(gt[0:nu, :], gt[0:nu, :], ACT.Exp).then_inc(gate_e, 1)
                    if nv:
                        diagonals(LEAD, tv_)
                    if nu:
                        act.wait_ge(act_in, j + 1)
                        nc.scalar.activation(au[:, 0:tu * UNR], au[:, 0:tu * UNR], ACT.Gelu).then_inc(gelu_out, 1)
                    if nv:
                        act.wait_ge(var_out, 2 * (j - 1) + 1)
                        nc.scalar.activation(junk[0:nv, :], rr[0:nv, :], ACT.Square, bias=st[0:nv, 1:2], accum_out=st[0:nv, 2:3]
                                             ).then_inc(squares, 1)
                        act.wait_ge(var_out, 2 * (j - 1) + 2)
                        nc.scalar.activation(st[0:nv, 4:5], st[0:nv, 3:4], ACT.Sqrt).then_inc(root_out, 1)
                act.wait_ge(const_in, 96)
                steps(act, step)

            @block.vector
            def _(dve):
                v = nc.vector
                dve.sem_inc(handed, 1)
                dve.sem_inc(u_used, UNR)
                dve.wait_ge(const_in, 96)

                def top16(n, src, count, vals, idx):
                    for i in range(count):
                        v.max(vals[0:n, i, 0:8], src(i))
                    dve.drain()
                    for i in range(count):
                        v.max_index(idx[0:n, i, 0:8], vals[0:n, i, 0:8], src(i))
                    dve.drain()
                    for i in range(count):
                        v.match_replace(src(i), vals[0:n, i, 0:8], src(i), LOW)
                    dve.drain()
                    for i in range(count):
                        v.max(vals[0:n, i, 8:16], src(i))
                    dve.drain()
                    for i in range(count):
                        v.max_index(idx[0:n, i, 8:16], vals[0:n, i, 8:16], src(i))
                    dve.drain()

                def step(j, n, nv, tu, tv_):
                    if n:
                        four = [n, PH, TOPK, TOPK]
                        dve.wait_ge(s_copied, j + 1)
                        dve.wait_ge(q_in, 32 * j + (32 if n == P else 48))
                        tl.hold(dve, "i_dve")
                        top16(n, lambda i: s1[0:n, i, :], S, tv, ti)
                        v.tensor_copy(tf[0:n, :, :], ti[0:n, :, :])
                        halves = tv[0:n, :, :].rearrange("p (h k) a -> p h k a", k=2)
                        cand = s1[0:n, :, :].rearrange("p (h k) (a b) -> p h (k a) b", k=2, b=TOPK)
                        v.tensor_tensor(cand, halves[:, :, 0, :].unsqueeze(3).to_broadcast(four),
                                        halves[:, :, 1, :].unsqueeze(2).to_broadcast(four), ALU.add)
                        dve.drain()
                        top16(n, lambda i: s1[0:n, 2 * i:2 * i + 2, :].rearrange("p a b -> p (a b)"), PH, bv, bi)
                        gv = gt[0:n, :].rearrange("p (h k) -> p h k", h=PH)
                        v.tensor_tensor(gv, bv[0:n, :, :], bv[0:n, :, 0:1].to_broadcast([n, PH, TOPK]), ALU.subtract).then_inc(best, 1)
                        for half in range(2):
                            if half == 0:
                                v.tensor_scalar(ba[0:n, :, :], bi[0:n, :, :], 4, None, ALU.logical_shift_right)
                            else:
                                v.tensor_scalar(ba[0:n, :, :], bi[0:n, :, :], 15, None, ALU.bitwise_and)
                            dve.drain()
                            v.tensor_copy(bf[0:n, half, :, :], ba[0:n, :, :])
                            dve.drain()
                            v.tensor_tensor(eq[0:n, :, :, :], iota[0:n, :].unsqueeze(1).unsqueeze(1).to_broadcast(four),
                                            bf[0:n, half, :, :].unsqueeze(3).to_broadcast(four), ALU.is_equal)
                            dve.drain()
                            tfh = tf[0:n, :, :].rearrange("p (h k) a -> p h k a", k=2)[:, :, half, :]
                            v.tensor_tensor(eq[0:n, :, :, :], eq[0:n, :, :, :], tfh.unsqueeze(2).to_broadcast(four), ALU.mult)
                            dve.drain()
                            v.tensor_reduce(ex[0:n, half, :], eq[0:n, :, :, :].rearrange("p h k a -> p (h k) a"), AX, ALU.add)
                            dve.drain()
                        v.scalar_tensor_tensor(ei[0:n, :], ex[0:n, 0, :], float(NK), ex[0:n, 1, :], ALU.mult, ALU.add).then_inc(index_out, 1)
                        dve.wait_ge(gate_e, j + 1)
                        v.tensor_reduce(sm[0:n, 0, :], gv, AX, ALU.add)
                        dve.drain()
                        v.reciprocal(sm[0:n, 1, :], sm[0:n, 0, :])
                        dve.drain()
                        v.tensor_tensor(gv, gv, sm[0:n, 1, :].unsqueeze(2).to_broadcast([n, PH, TOPK]), ALU.mult)
                        dve.drain().then_inc(gates_out, 1)
                        with dve.Fori(0, tu) as c:
                            for u in range(UNR):
                                dve.wait_ge(u_in[u], 16 * (TURNS * j + c) + 16)
                                tl.hold(dve, "i_dve")
                                v.tensor_tensor_reduce(urow[:, u, :], urow[:, u, :], x1[:, :], 1.0, 0.0, ALU.mult, ALU.add,
                                                       as_[:, u:u + 1]).then_inc(u_used, 1)
                            dve.drain()
                            v.tensor_copy(au[:, ds(c * UNR, UNR)], as_[:, :])
                            dve.drain()
                        dve.drain().then_inc(act_in, 1)
                    if nv:
                        dve.wait_ge(v_used, PICKS * (j - 1) + tv_ * UNR + VR)
                        dve.wait_ge(stored, 16 * (j - 1) + 16)
                        v.scalar_tensor_tensor(rr[0:nv, :], ax[0:nv, :], 1.0, p_f[0:nv, :, :].rearrange("p a n -> p (a n)"),
                                               ALU.mult, ALU.add, accum_out=st[0:nv, 0:1])
                        dve.drain()
                    if n:
                        dve.wait_ge(gelu_out, j + 1)
                        if n < P:
                            dve.wait_ge(moved_g, 16)
                        v.tensor_tensor(cf[:, 0:tu * UNR], au[:, 0:tu * UNR], gt[:, 0:tu * UNR], ALU.mult)
                        v.tensor_copy(ew[:, 0:tu * UNR], ei[:, 0:tu * UNR])
                        v.tensor_scalar(ax[0:n, :], x1[0:n, :], ALPHA, None, ALU.mult)
                        dve.drain().then_inc(handed, 1)
                    if nv:
                        layer_norm_steps(nc, dve, rr, gb, st, nv, j - 1, squares, var_out, root_out)
                        dve.drain().then_inc(normed, 1)
                steps(dve, step)


OUTS = {"y": (T, D), "kT_out": (8, P, T), "v_tok": (T, DA), "logfT": (AH, T), "ssm_pT": (SG, P, 2 * P),
        "ssm_sT": (SG, P, NB, 2 * P), "convT": (SG, P, 4 * 27)}
SCRATCH = {"uT": (NT, P, T), "cum": (AH, T), "ncum": (AH, T), "cs": (SH, T), "facg": (SG, P, 60), "mT": (KT, P, T),
           "attT": (8, P, T), "mixT": (KT, P, T), "x1": (T, D), "x1T": (KT, P, T), "qT": (KT, P, T)}


def build(nc, io, dr):
    dr = dict(dr)
    dr["v_heads"] = dr["v_tok"].rearrange("t (h d) -> h t d", d=DH)
    dr["attT_heads"] = dr["attT"].rearrange("a (h p) n -> (a h) p n", p=DH)
    whole = ExitStack()
    tl = Tools(nc, whole)
    for stage in (project_in, gate_scalars, mamba, prompt_attention, sample_attention, merge, out_norm, queries, peer):
        tl.run(stage, io, dr)
    whole.close()


def kernel(**inputs):
    import numpy as np
    import concourse.bacc as bacc
    from concourse import mybir as mb
    from concourse.bass_utils import run_bass_kernel_spmd as run

    a = {k: np.asarray(v) for k, v in inputs.items()}
    f32 = np.float32
    x = np.concatenate([a["x_prompt"].reshape(TP, D), a["x_sample"].reshape(TS, D)])

    def tiles(w):
        r, c = w.shape
        return w.reshape(r // P, P, c // P, P).transpose(2, 1, 0, 3)

    w_in = a["w_in"][0]
    cut = np.cumsum([0, DA, DA, DA, AH, D, 4096, SH, D, D])
    q, k, v, fg, z, xbc, dt, ga, gs = (w_in[:, cut[i]:cut[i + 1]] for i in range(9))
    zeros = lambda *s: np.zeros(s, f32)
    misc = np.concatenate([fg, zeros(D, 16), dt, zeros(D, 64)], axis=1)
    w_all = np.concatenate([q, k, z, xbc, ga, gs, misc], axis=1)

    def group4(w):
        t = w.reshape((32, P) + w.shape[1:])
        pick = np.array([[2 * g, 2 * g + 1, 16 + g, 24 + g] for g in range(SG)])
        return np.moveaxis(t[pick], 2, 1)
    pairs = lambda w: w.reshape(SG, 2, P).transpose(0, 2, 1)
    group_par = np.concatenate([group4(a["conv_w"][0].T).reshape(SG, P, 16), group4(a["conv_b"][0]).reshape(SG, P, 4),
                                pairs(np.repeat(a["d_skip"][0], 64)), pairs(a["ssm_norm_w"][0])], axis=2)
    gate_par = zeros(64, 2)
    gate_par[0:AH, 0] = a["b_fgate"][0]
    gate_par[32:64, 0] = a["dt_bias"][0]
    gate_par[32:64, 1] = a["a_log"][0]
    back = lambda c: c[:, ::-1]
    pool = a["cache_k"].shape[1]
    cache_k = back(a["cache_k"][0]).reshape(pool, PAGE, 8, P).transpose(0, 3, 2, 1).reshape(pool * P, DA)
    cache_v = back(a["cache_v"][0]).reshape(pool * PAGE, DA)
    cache_f = back(a["cache_logf"][0]).transpose(0, 2, 1).reshape(pool * AH, PAGE)

    t = np.arange(T)
    reset = np.ones((64, T), f32)
    reset[:, TP::TB] = 0
    reset[32:, 0:TP:P] = 0
    i, j = np.arange(P)[:, None], np.arange(P)[None, :]
    mask_st = np.where(j >= i, 0, NEG).astype(f32)
    i8, j8 = np.arange(TS)[:, None], np.arange(TS)[None, :]
    mask_ss = np.where((j8 >= i8) & (j8 // TB == i8 // TB), 0, NEG).astype(f32)
    mask_qk = np.where(j <= i, 0, NEG).astype(f32)
    mask_new = np.where(np.arange(TB)[None, :] <= (np.arange(P) % TB)[:, None], 0, NEG).astype(f32)
    arrays = {
        "xT": x.T.reshape(KT, P, T).transpose(1, 0, 2), "x_tok": x, "w_in": tiles(w_all),
        "w_v": v.reshape(KT, P, 2, 512).transpose(2, 1, 0, 3), "gate_par": gate_par, "reset": reset,
        "ident": np.eye(P, dtype=f32), "ones": np.ones((P, P), f32), "ones_row": np.ones((1, T), f32),
        "mask_st": mask_st, "mask_ss": mask_ss, "mask_qk": mask_qk, "mask_new": mask_new,
        "seqm": (np.arange(TS)[:, None] // TB == np.arange(NB)[None, :]).astype(f32),
        "sel_hq": (np.arange(AH)[:, None] == np.arange(P)[None, :] // TB).astype(f32),
        "fold": (i % TS == j % TS).astype(f32),
        "iota16": np.broadcast_to(np.arange(TOPK, dtype=f32), (P, TOPK)),
        "conv_old": group4(a["state_conv"][0].transpose(2, 0, 1)).reshape(SG, P, 4 * NB * 3),
        "group_par": group_par,
        "ssm_old": a["state_ssm"][0].reshape(NB, SG, 2 * P, SN).transpose(1, 3, 0, 2),
        "cache_k": cache_k, "cache_v": cache_v, "cache_f": cache_f, "pages": a["page_table"][:, ::-1],
        "w_ba": tiles(a["w_br_att"][0]), "w_bs": tiles(a["w_br_ssm"][0]),
        "w_out": a["w_out"][0].reshape(KT, P, D).transpose(1, 0, 2), "w_query": tiles(a["w_query"][0]),
        "keysT": a["sub_keys"][0].reshape(2 * PH, NK, P).transpose(2, 0, 1),
        "expert_u": a["expert_u"][0], "expert_v": a["expert_v"][0],
        "ln1_g": a["ln1_g"], "ln1_b": a["ln1_b"], "ln2_g": a["ln2_g"], "ln2_b": a["ln2_b"],
    }
    arrays = {n: np.ascontiguousarray(w) for n, w in arrays.items()}
    nc = bacc.Bacc("TRN2", target_bir_lowering=False, num_devices=1)
    io = {n: nc.dram_tensor("in_" + n, w.shape, mb.dt.from_np(w.dtype), kind="ExternalInput").ap() for n, w in arrays.items()}
    dr = {n: nc.dram_tensor("out_" + n, s, F32, kind="ExternalOutput").ap() for n, s in OUTS.items()}
    dr.update({n: nc.dram_tensor("tmp_" + n, s, F32, kind="Internal").ap() for n, s in SCRATCH.items()})
    build(nc, io, dr)
    r = run(nc, [{"in_" + n: w for n, w in arrays.items()}], core_ids=[0]).results[0]
    o = {n: np.asarray(r["out_" + n]) for n in OUTS}
    kk = o["kT_out"].reshape(DA, T).T
    vv, lf = o["v_tok"], o["logfT"].T
    ssm_p = o["ssm_pT"].transpose(0, 2, 1).reshape(1, 1, SH, 64, SN)
    ssm_s = o["ssm_sT"].transpose(2, 0, 3, 1).reshape(1, NB, SH, 64, SN)
    order = np.argsort(np.array([[2 * g, 2 * g + 1, 16 + g, 24 + g] for g in range(SG)]).ravel())
    conv = o["convT"].reshape(SG, P, 4, 27).transpose(0, 2, 1, 3).reshape(32, P, 27)[order].reshape(4096, 27).T
    c = np.ascontiguousarray
    return (c(o["y"][:TP].reshape(1, TP, D)), c(o["y"][TP:].reshape(NB, TB, D)),
            c(kk[:TP].reshape(1, 1, TP, AH, DH)), c(vv[:TP].reshape(1, 1, TP, AH, DH)), c(lf[:TP].reshape(1, 1, TP, AH)),
            c(ssm_p), c(conv[:3].reshape(1, 1, 3, 4096)),
            c(kk[TP:].reshape(1, NB, TB, AH, DH)), c(vv[TP:].reshape(1, NB, TB, AH, DH)), c(lf[TP:].reshape(1, NB, TB, AH)),
            c(ssm_s), c(conv[3:].reshape(1, NB, 3, 4096)))
```
